# Optimizing a Trainium2 kernel written in Bass

```python
import jax
import jax.numpy as jnp
from jax import lax
import numpy as np
import math
import jax, jax.numpy as jnp

D_MODEL = 1024
BATCH = 1
SEQ = 512
DEPTH = 1

D_MIX = D_MODEL
SB_HEAD_DIM = 64
D_SB = D_MIX // 2
SB_HEADS = D_SB // SB_HEAD_DIM
BLOCK_Q = 128
D_LRU = D_MIX // 4
LRU_BLOCKS = 4
LRU_BLOCK = D_LRU // LRU_BLOCKS
LRU_CONV_WIDTH = 4
LRU_C = 8.0
D_CONF = D_MIX // 4
CONF_CONV_WIDTH = 31
D_IN = 3 * D_SB + 2 * D_LRU + 2 * D_CONF
N_GROUPS = 4
EXPERTS_PER_GROUP = 8
N_EXPERTS = N_GROUPS * EXPERTS_PER_GROUP
TOP_K_FINE = 2
D_EXPERT = D_MODEL // 2
MOE_BLOCK = 256
EPS = 1e-6


def rms_norm(x, g):
    xf = x.astype(jnp.float32)
    y = xf * lax.rsqrt(jnp.mean(xf * xf, axis=-1, keepdims=True) + EPS)
    return (y * g.astype(jnp.float32)).astype(x.dtype)

def layer_norm(x, g, b):
    xf = x.astype(jnp.float32)
    mu = jnp.mean(xf, axis=-1, keepdims=True)
    xc = xf - mu
    var = jnp.mean(xc * xc, axis=-1, keepdims=True)
    return xc * lax.rsqrt(var + EPS) * g.astype(jnp.float32) + b.astype(jnp.float32)

def causal_depthwise_conv(x, w, b):
    k_width, chans = w.shape
    y = lax.conv_general_dilated(
        x, w.astype(x.dtype)[:, None, :], window_strides=(1,),
        padding=[(k_width - 1, 0)], dimension_numbers=('NWC', 'WIO', 'NWC'),
        feature_group_count=chans)
    return y + b.astype(x.dtype)

def stick_breaking_attention(q, k, v):
    seq = q.shape[2]
    scale = SB_HEAD_DIM ** -0.5
    outs = []
    for i in range(seq // BLOCK_Q):
        q0 = i * BLOCK_Q
        kv_len = q0 + BLOCK_Q
        qb = q[:, :, q0:kv_len]
        kb = k[:, :, :kv_len]
        vb = v[:, :, :kv_len]
        z = jnp.einsum('bhqd,bhkd->bhqk', qb, kb, preferred_element_type=jnp.float32) * scale
        t_pos = q0 + jnp.arange(BLOCK_Q, dtype=jnp.int32)[:, None]
        s_pos = jnp.arange(kv_len, dtype=jnp.int32)[None, :]
        mask = s_pos < t_pos
        log_keep = jnp.where(mask, jax.nn.log_sigmoid(-z), 0.0)
        suffix = lax.cumsum(log_keep, axis=3, reverse=True) - log_keep
        wts = jnp.where(mask, jnp.exp(jax.nn.log_sigmoid(z) + suffix), 0.0)
        outs.append(jnp.einsum('bhqk,bhkd->bhqd', wts.astype(vb.dtype), vb))
    return jnp.concatenate(outs, axis=2)

def _linear_combine(c1, c2):
    a1, b1 = c1
    a2, b2 = c2
    return a1 * a2, a2 * b1 + b2

def rg_lru_branch(xr, xg, conv_w, conv_b, wa, ba, wx, bx, lam):
    f32 = jnp.float32
    bsz, seq, _ = xr.shape
    xr = causal_depthwise_conv(xr, conv_w, conv_b)
    xblk = xr.reshape(bsz, seq, LRU_BLOCKS, LRU_BLOCK)
    gate_r = jnp.einsum('bsnc,ncd->bsnd', xblk, wa).reshape(bsz, seq, D_LRU) + ba
    gate_i = jnp.einsum('bsnc,ncd->bsnd', xblk, wx).reshape(bsz, seq, D_LRU) + bx
    log_a = LRU_C * jax.nn.sigmoid(gate_r.astype(f32)) * jax.nn.log_sigmoid(lam.astype(f32))
    a = jnp.exp(log_a)
    u = jnp.sqrt(-jnp.expm1(2.0 * log_a)) * (jax.nn.sigmoid(gate_i.astype(f32)) * xr.astype(f32))
    _, h = lax.associative_scan(_linear_combine, (a, u), axis=1)
    return (h * jax.nn.gelu(xg.astype(f32))).astype(xr.dtype)

def conformer_conv(xc, dw_w, dw_b, ln_g, ln_b, pw_w, pw_b):
    val, gate = jnp.split(xc, 2, axis=-1)
    u = val * jax.nn.sigmoid(gate)
    u = causal_depthwise_conv(u, dw_w, dw_b)
    u = jax.nn.silu(layer_norm(u, ln_g, ln_b)).astype(xc.dtype)
    return jnp.einsum('bsc,ce->bse', u, pw_w) + pw_b

def hierarchical_moe(h, w_coarse, w_fine, w_gate, w_up, w_down):
    n_tok, d = h.shape
    f32 = jnp.float32
    logits_c = jnp.einsum('nd,dg->ng', h, w_coarse, preferred_element_type=f32)
    probs_c = jax.nn.softmax(logits_c, axis=-1)
    grp = jnp.argmax(logits_c, axis=-1).astype(jnp.int32)
    w_grp = jnp.take_along_axis(probs_c, grp[:, None], axis=-1)
    logits_f = jnp.einsum('nd,de->ne', h, w_fine, preferred_element_type=f32)
    logits_f = logits_f.reshape(n_tok, N_GROUPS, EXPERTS_PER_GROUP)
    logits_f = jnp.take_along_axis(logits_f, grp[:, None, None], axis=1)[:, 0]
    top_val, top_idx = lax.top_k(logits_f, TOP_K_FINE)
    gate = (jax.nn.softmax(top_val, axis=-1) * w_grp).astype(h.dtype)
    expert = grp[:, None] * EXPERTS_PER_GROUP + top_idx.astype(jnp.int32)

    n_asg = n_tok * TOP_K_FINE
    flat_e = expert.reshape(n_asg)
    flat_tok = jnp.repeat(jnp.arange(n_tok, dtype=jnp.int32), TOP_K_FINE)
    flat_gate = gate.reshape(n_asg)
    order = jnp.argsort(flat_e)
    sorted_e = flat_e[order]
    counts = jnp.bincount(flat_e, length=N_EXPERTS).astype(jnp.int32)
    padded = (counts + MOE_BLOCK - 1) // MOE_BLOCK * MOE_BLOCK
    starts = jnp.cumsum(counts) - counts
    padded_ends = jnp.cumsum(padded)
    padded_starts = padded_ends - padded
    dest = padded_starts[sorted_e] + jnp.arange(n_asg, dtype=jnp.int32) - starts[sorted_e]
    n_blocks = -(-n_asg // MOE_BLOCK) + N_EXPERTS
    n_slots = n_blocks * MOE_BLOCK
    slot_tok = jnp.full((n_slots,), n_tok, jnp.int32).at[dest].set(flat_tok[order])
    slot_gate = jnp.zeros((n_slots,), h.dtype).at[dest].set(flat_gate[order])
    block_start = jnp.arange(n_blocks, dtype=jnp.int32) * MOE_BLOCK
    block_e = jnp.minimum(jnp.searchsorted(padded_ends, block_start, side='right'),
                          N_EXPERTS - 1).astype(jnp.int32)
    h_pad = jnp.concatenate([h, jnp.zeros((1, d), h.dtype)], axis=0)
    xb = h_pad[slot_tok].reshape(n_blocks, MOE_BLOCK, d)

    def run_block(args):
        xe, e = args
        return (jax.nn.silu(xe @ w_gate[e]) * (xe @ w_up[e])) @ w_down[e]

    yb = lax.map(run_block, (xb, block_e)).reshape(n_slots, d)
    y = jnp.zeros((n_tok + 1, d), yb.dtype).at[slot_tok].add(yb * slot_gate[:, None])
    return y[:n_tok]

def first_inputs(seed: int = 0) -> dict:
    key = jax.random.key(seed)
    ks = jax.random.split(key, 28)
    f32 = jnp.float32
    L = DEPTH

    def nrm(k, shape, scale):
        return jax.random.normal(k, shape, f32) * scale

    def gain(k, shape):
        return 1.0 + 0.05 * jax.random.normal(k, shape, f32)

    a_c = jax.random.uniform(ks[11], (L, D_LRU), f32, 0.9, 0.999)
    a0 = a_c ** (1.0 / LRU_C)
    lam = jnp.log(a0) - jnp.log1p(-a0)

    return {
        'x': jax.random.normal(ks[0], (BATCH, SEQ, D_MODEL), f32),
        'norm1_g': gain(ks[1], (L, D_MODEL)),
        'w_in': nrm(ks[2], (L, D_MODEL, D_IN), D_MODEL ** -0.5),
        'q_norm_g': gain(ks[3], (L, SB_HEAD_DIM)),
        'k_norm_g': gain(ks[4], (L, SB_HEAD_DIM)),
        'lru_conv_w': nrm(ks[5], (L, LRU_CONV_WIDTH, D_LRU), LRU_CONV_WIDTH ** -0.5),
        'lru_conv_b': nrm(ks[6], (L, D_LRU), 0.02),
        'lru_wa': nrm(ks[7], (L, LRU_BLOCKS, LRU_BLOCK, LRU_BLOCK), LRU_BLOCK ** -0.5),
        'lru_ba': nrm(ks[8], (L, D_LRU), 0.02),
        'lru_wx': nrm(ks[9], (L, LRU_BLOCKS, LRU_BLOCK, LRU_BLOCK), LRU_BLOCK ** -0.5),
        'lru_bx': nrm(ks[10], (L, D_LRU), 0.02),
        'lru_lambda': lam,
        'conf_dw_w': nrm(ks[12], (L, CONF_CONV_WIDTH, D_CONF), CONF_CONV_WIDTH ** -0.5),
        'conf_dw_b': nrm(ks[13], (L, D_CONF), 0.02),
        'conf_ln_g': gain(ks[14], (L, D_CONF)),
        'conf_ln_b': nrm(ks[15], (L, D_CONF), 0.02),
        'conf_pw_w': nrm(ks[16], (L, D_CONF, D_CONF), D_CONF ** -0.5),
        'conf_pw_b': nrm(ks[17], (L, D_CONF), 0.02),
        'out_norm_g': gain(ks[18], (L, D_MIX)),
        'w_out': nrm(ks[19], (L, D_MIX, D_MODEL), D_MIX ** -0.5),
        'norm2_g': gain(ks[20], (L, D_MODEL)),
        'router_coarse': nrm(ks[21], (L, D_MODEL, N_GROUPS), D_MODEL ** -0.5),
        'router_fine': nrm(ks[22], (L, D_MODEL, N_EXPERTS), D_MODEL ** -0.5),
        'exp_w_gate': nrm(ks[23], (L, N_EXPERTS, D_MODEL, D_EXPERT), D_MODEL ** -0.5),
        'exp_w_up': nrm(ks[24], (L, N_EXPERTS, D_MODEL, D_EXPERT), D_MODEL ** -0.5),
        'exp_w_down': nrm(ks[25], (L, N_EXPERTS, D_EXPERT, D_MODEL), D_EXPERT ** -0.5),
    }

def first_block(x, norm1_g, w_in, q_norm_g, k_norm_g, lru_conv_w, lru_conv_b, lru_wa, lru_ba,
              lru_wx, lru_bx, lru_lambda, conf_dw_w, conf_dw_b, conf_ln_g, conf_ln_b,
              conf_pw_w, conf_pw_b, out_norm_g, w_out, norm2_g, router_coarse, router_fine,
              exp_w_gate, exp_w_up, exp_w_down):
    bsz, seq, d = x.shape
    splits = [D_SB, 2 * D_SB, 3 * D_SB, 3 * D_SB + D_LRU, 3 * D_SB + 2 * D_LRU]
    for l in range(DEPTH):
        h = rms_norm(x, norm1_g[l])
        proj = jnp.einsum('bsd,de->bse', h, w_in[l])
        q, k, v, xr, xg, xc = jnp.split(proj, splits, axis=-1)
        q = rms_norm(q.reshape(bsz, seq, SB_HEADS, SB_HEAD_DIM), q_norm_g[l]).transpose(0, 2, 1, 3)
        k = rms_norm(k.reshape(bsz, seq, SB_HEADS, SB_HEAD_DIM), k_norm_g[l]).transpose(0, 2, 1, 3)
        v = v.reshape(bsz, seq, SB_HEADS, SB_HEAD_DIM).transpose(0, 2, 1, 3)
        y_a = stick_breaking_attention(q, k, v).transpose(0, 2, 1, 3).reshape(bsz, seq, D_SB)
        y_b = rg_lru_branch(xr, xg, lru_conv_w[l], lru_conv_b[l], lru_wa[l], lru_ba[l],
                            lru_wx[l], lru_bx[l], lru_lambda[l])
        y_c = conformer_conv(xc, conf_dw_w[l], conf_dw_b[l], conf_ln_g[l], conf_ln_b[l],
                             conf_pw_w[l], conf_pw_b[l])
        g_out = out_norm_g[l]
        y = jnp.concatenate([
            rms_norm(y_a, g_out[:D_SB]),
            rms_norm(y_b, g_out[D_SB:D_SB + D_LRU]),
            rms_norm(y_c, g_out[D_SB + D_LRU:]),
        ], axis=-1)
        x = x + jnp.einsum('bse,ed->bsd', y, w_out[l])
        h2 = rms_norm(x, norm2_g[l]).reshape(bsz * seq, d)
        x = x + hierarchical_moe(h2, router_coarse[l], router_fine[l], exp_w_gate[l],
                                 exp_w_up[l], exp_w_down[l]).reshape(bsz, seq, d)
    return x


CTX_LEN = 256
GRID_W = 64
MIX_W = D_MODEL
F_W = MIX_W // 2
F_GROUPS = 4
F_GROUP_W = F_W // F_GROUPS
DN_W = MIX_W - F_W
DN_HEADS = 4
DK = DN_W // DN_HEADS
DV = DN_W // DN_HEADS
QK_W = DN_HEADS * DK
V_W = DN_HEADS * DV
CONV_CH = 2 * QK_W + V_W
W_IN = F_W + CONV_CH + V_W + 4 * DN_HEADS
CONV_K = 3
CHUNK = 64
N_EXPERTS_2 = N_GROUPS * EXPERTS_PER_GROUP
TOP_K = 2
D_EXPERT_2 = D_MODEL // 2
MOE_BLOCK_2 = 128


def rmsnorm(x, g):
    xf = x.astype(jnp.float32)
    y = xf * lax.rsqrt(jnp.mean(xf * xf, axis=-1, keepdims=True) + EPS) * g.astype(jnp.float32)
    return y.astype(x.dtype)

def l2norm(a):
    af = a.astype(jnp.float32)
    return af * lax.rsqrt(jnp.sum(af * af, axis=-1, keepdims=True) + EPS)

def modulate(h, shift, scale):
    return h * (1 + scale) + shift

def conv_grid(u, w):
    b, t, ch = u.shape
    rows = t // GRID_W
    y = lax.conv_general_dilated(u.reshape(b, rows, GRID_W, ch), w[:, :, None, :].astype(u.dtype),
                                 (1, 1), 'SAME', dimension_numbers=('NHWC', 'HWIO', 'NHWC'),
                                 feature_group_count=ch)
    return y.reshape(b, t, ch)

def conv_seq(u, w):
    ch = u.shape[-1]
    return lax.conv_general_dilated(u, w[1][:, None, :].astype(u.dtype), (1,), 'SAME',
                                    dimension_numbers=('NWC', 'WIO', 'NWC'), feature_group_count=ch)

def fourier_mix(f):
    b, t, _ = f.shape
    fg = f.astype(jnp.float32).reshape(b, t, F_GROUPS, F_GROUP_W)
    out = jnp.fft.fft2(fg, axes=(1, 3), norm='ortho').real
    return out.reshape(b, t, F_W).astype(f.dtype)

def gated_delta_chunked(q, k, v, g, beta, s0):
    b, t, h, dk = q.shape
    dv = v.shape[-1]
    n = t // CHUNK

    def chunks(a):
        a = jnp.moveaxis(a.astype(jnp.float32), 2, 1)
        return a.reshape(b, h, n, CHUNK, *a.shape[3:])

    q = chunks(q) * dk ** -0.5
    k = chunks(k)
    v = chunks(v)
    beta = chunks(beta)
    gc = jnp.cumsum(chunks(g), axis=-1)
    idx = jnp.arange(CHUNK)
    lower = idx[:, None] >= idx[None, :]
    decay = jnp.exp(jnp.where(lower, gc[..., :, None] - gc[..., None, :], -jnp.inf))
    k_beta = k * beta[..., None]
    m = jnp.where(idx[:, None] > idx[None, :],
                  jnp.einsum('bhnid,bhnjd->bhnij', k_beta, k) * decay, 0.0)
    eye = jnp.eye(CHUNK, dtype=jnp.float32)
    a_mat = eye + m
    t_inv = lax.linalg.triangular_solve(a_mat, jnp.broadcast_to(eye, a_mat.shape), left_side=True,
                                        lower=True, unit_diagonal=True)
    u = t_inv @ (v * beta[..., None])
    w = t_inv @ (k_beta * jnp.exp(gc)[..., None])
    intra = jnp.einsum('bhnid,bhnjd->bhnij', q, k) * decay

    def step(s, blk):
        q_i, k_i, u_i, w_i, a_i, g_i = blk
        v_new = u_i - w_i @ s
        o_i = (q_i * jnp.exp(g_i)[..., None]) @ s + a_i @ v_new
        g_last = g_i[..., -1:]
        s = s * jnp.exp(g_last)[..., None] + jnp.einsum(
            'bhcd,bhce->bhde', k_i * jnp.exp(g_last - g_i)[..., None], v_new)
        return s, o_i

    xs = tuple(jnp.moveaxis(a, 2, 0) for a in (q, k, u, w, intra, gc))
    s_final, o = lax.scan(step, s0.astype(jnp.float32), xs)
    o = jnp.moveaxis(o, 0, 2).reshape(b, h, t, dv)
    return jnp.moveaxis(o, 1, 2), s_final

def bidir_delta(q, k, v, g, beta, s0_fwd, s0_bwd):
    flip = lambda a: jnp.flip(a, axis=1)
    o_f, s_f = gated_delta_chunked(q, k, v, g[:, :, 0], beta[:, :, 0], s0_fwd)
    o_b, s_b = gated_delta_chunked(flip(q), flip(k), flip(v), flip(g[:, :, 1]), flip(beta[:, :, 1]), s0_bwd)
    return o_f + flip(o_b), s_f, s_b

def mixer_features(h, w_in, conv_w, a_log, dt_bias, conv_fn):
    b, t = h.shape[:2]
    p = h @ w_in
    f, qkv, z, gates = jnp.split(p, [F_W, F_W + CONV_CH, F_W + CONV_CH + V_W], axis=-1)
    qkv = jax.nn.silu(conv_fn(qkv, conv_w))
    q, k, v = jnp.split(qkv, [QK_W, 2 * QK_W], axis=-1)
    q = l2norm(q.reshape(b, t, DN_HEADS, DK))
    k = l2norm(k.reshape(b, t, DN_HEADS, DK))
    v = v.reshape(b, t, DN_HEADS, DV)
    gates = gates.astype(jnp.float32).reshape(b, t, 2, 2, DN_HEADS)
    beta = jax.nn.sigmoid(gates[:, :, 0])
    g = -jnp.exp(a_log.astype(jnp.float32)) * jax.nn.softplus(gates[:, :, 1] + dt_bias.astype(jnp.float32))
    return f, q, k, v, z, g, beta

def mixer_output(f, o, z, onorm_g, w_out):
    b, t = f.shape[:2]
    o = (rmsnorm(o, onorm_g) * jax.nn.silu(z.reshape(b, t, DN_HEADS, DV))).astype(f.dtype)
    return jnp.concatenate([fourier_mix(f), o.reshape(b, t, V_W)], axis=-1) @ w_out

def moe_ffn(h, w_group, b_group, w_router, b_router, w_gate, w_up, w_down):
    shp = h.shape
    d = shp[-1]
    xf = h.reshape(-1, d)
    n = xf.shape[0]
    pg = jax.nn.softmax((xf @ w_group).astype(jnp.float32) + b_group.astype(jnp.float32), axis=-1)
    pg_top, g_top = lax.top_k(pg, 1)
    el = ((xf @ w_router).astype(jnp.float32) + b_router.astype(jnp.float32)).reshape(
        n, N_GROUPS, EXPERTS_PER_GROUP)
    el_g = el[jnp.arange(n), g_top[:, 0]]
    pe_top, e_top = lax.top_k(jax.nn.softmax(el_g, axis=-1), TOP_K)
    wts = pg_top * pe_top / jnp.sum(pe_top, axis=-1, keepdims=True)
    eid = (g_top * EXPERTS_PER_GROUP + e_top).reshape(-1).astype(jnp.int32)
    w_f = wts.reshape(-1)
    n_assign = n * TOP_K
    order = jnp.argsort(eid)
    e_s = eid[order]
    tok_s = (order // TOP_K).astype(jnp.int32)
    w_s = w_f[order]
    counts = jnp.zeros((N_EXPERTS_2,), jnp.int32).at[eid].add(1)
    start = jnp.cumsum(counts) - counts
    pcounts = (counts + MOE_BLOCK_2 - 1) // MOE_BLOCK_2 * MOE_BLOCK_2
    pend = jnp.cumsum(pcounts)
    pstart = pend - pcounts
    dest = pstart[e_s] + (jnp.arange(n_assign, dtype=jnp.int32) - start[e_s])
    n_slots = -(-n_assign // MOE_BLOCK_2) * MOE_BLOCK_2 + N_EXPERTS_2 * MOE_BLOCK_2
    n_blocks = n_slots // MOE_BLOCK_2
    slot_tok = jnp.full((n_slots,), n, jnp.int32).at[dest].set(tok_s)
    slot_w = jnp.zeros((n_slots,), jnp.float32).at[dest].set(w_s)
    blk_expert = jnp.minimum(
        jnp.searchsorted(pend, jnp.arange(n_blocks, dtype=jnp.int32) * MOE_BLOCK_2, side='right'),
        N_EXPERTS_2 - 1)
    x_pad = jnp.concatenate([xf, jnp.zeros((1, d), xf.dtype)], axis=0)
    xs = x_pad[slot_tok].reshape(n_blocks, MOE_BLOCK_2, d)

    def expert_block(args):
        xb, e = args
        hid = jax.nn.silu(xb @ w_gate[e]) * (xb @ w_up[e])
        return hid @ w_down[e]

    ys = lax.map(expert_block, (xs, blk_expert)).reshape(n_slots, d)
    out = jnp.zeros((n + 1, d), ys.dtype).at[slot_tok].add(ys * slot_w[:, None].astype(ys.dtype))
    return out[:n].reshape(shp)

def trunk_layer(x, ctx, c, c_ctx, w_mod, b_mod, norm1_g, w_in, conv_w, a_log, dt_bias, onorm_g, w_out,
                norm2_g, w_group, b_group, w_router, b_router, w_gate, w_up, w_down, update_ctx):
    mod_x = jnp.split((jax.nn.silu(c) @ w_mod + b_mod)[:, None, :], 6, axis=-1)
    mod_c = jnp.split((jax.nn.silu(c_ctx) @ w_mod + b_mod)[None, None, :], 6, axis=-1)

    hc = modulate(rmsnorm(ctx, norm1_g), mod_c[0], mod_c[1])
    fc, qc, kc, vc, zc, gc, bc = mixer_features(hc, w_in, conv_w, a_log, dt_bias, conv_seq)
    zero_state = jnp.zeros((ctx.shape[0], DN_HEADS, DK, DV), jnp.float32)
    oc, s_fwd, s_bwd = bidir_delta(qc, kc, vc, gc, bc, zero_state, zero_state)

    hx = modulate(rmsnorm(x, norm1_g), mod_x[0], mod_x[1])
    fx, qx, kx, vx, zx, gx, bx = mixer_features(hx, w_in, conv_w, a_log, dt_bias, conv_grid)
    ox, _, _ = bidir_delta(qx, kx, vx, gx, bx, s_fwd, s_bwd)
    x = x + mod_x[2] * mixer_output(fx, ox, zx, onorm_g, w_out)
    x = x + mod_x[5] * moe_ffn(modulate(rmsnorm(x, norm2_g), mod_x[3], mod_x[4]),
                               w_group, b_group, w_router, b_router, w_gate, w_up, w_down)
    if update_ctx:
        ctx = ctx + mod_c[2] * mixer_output(fc, oc, zc, onorm_g, w_out)
        ctx = ctx + mod_c[5] * moe_ffn(modulate(rmsnorm(ctx, norm2_g), mod_c[3], mod_c[4]),
                                       w_group, b_group, w_router, b_router, w_gate, w_up, w_down)
    return x, ctx

def second_inputs(seed: int = 0) -> dict:
    key = jax.random.key(seed)
    ks = jax.random.split(key, 24)
    nrm = lambda k, shape, s: jax.random.normal(k, shape, jnp.float32) * s
    x = nrm(ks[0], (BATCH, SEQ, D_MODEL), 1.0)
    c = nrm(ks[1], (BATCH, D_MODEL), 1.0)
    ctx = nrm(ks[2], (BATCH, CTX_LEN, D_MODEL), 1.0)
    c_ctx = nrm(ks[3], (D_MODEL,), 1.0)
    w_mod = nrm(ks[4], (DEPTH, D_MODEL, 6 * D_MODEL), 0.5 * D_MODEL ** -0.5)
    b_mod = nrm(ks[5], (DEPTH, 6 * D_MODEL), 0.01)
    norm1_g = 1.0 + nrm(ks[6], (DEPTH, D_MODEL), 0.02)
    w_in = nrm(ks[7], (DEPTH, D_MODEL, W_IN), D_MODEL ** -0.5)
    conv_w = nrm(ks[8], (DEPTH, CONV_K, CONV_K, CONV_CH), 1.0 / CONV_K)
    a_log = jnp.log(jax.random.uniform(ks[9], (DEPTH, 2, DN_HEADS), jnp.float32, 1.0, 16.0))
    dt = jnp.exp(jax.random.uniform(ks[10], (DEPTH, 2, DN_HEADS), jnp.float32,
                                    math.log(1e-3), math.log(1e-1)))
    dt_bias = dt + jnp.log(-jnp.expm1(-dt))
    onorm_g = 1.0 + nrm(ks[11], (DEPTH, DV), 0.02)
    w_out = nrm(ks[12], (DEPTH, MIX_W, D_MODEL), MIX_W ** -0.5)
    norm2_g = 1.0 + nrm(ks[13], (DEPTH, D_MODEL), 0.02)
    w_group = nrm(ks[14], (DEPTH, D_MODEL, N_GROUPS), D_MODEL ** -0.5)
    b_group = nrm(ks[15], (DEPTH, N_GROUPS), 0.01)
    w_router = nrm(ks[16], (DEPTH, D_MODEL, N_EXPERTS_2), D_MODEL ** -0.5)
    b_router = nrm(ks[17], (DEPTH, N_EXPERTS_2), 0.01)
    w_gate = nrm(ks[18], (DEPTH, N_EXPERTS_2, D_MODEL, D_EXPERT_2), D_MODEL ** -0.5)
    w_up = nrm(ks[19], (DEPTH, N_EXPERTS_2, D_MODEL, D_EXPERT_2), D_MODEL ** -0.5)
    w_down = nrm(ks[20], (DEPTH, N_EXPERTS_2, D_EXPERT_2, D_MODEL), D_EXPERT_2 ** -0.5)
    final_g = 1.0 + nrm(ks[21], (D_MODEL,), 0.02)
    return {"x": x, "c": c, "ctx": ctx, "c_ctx": c_ctx, "w_mod": w_mod, "b_mod": b_mod,
            "norm1_g": norm1_g, "w_in": w_in, "conv_w": conv_w, "a_log": a_log, "dt_bias": dt_bias,
            "onorm_g": onorm_g, "w_out": w_out, "norm2_g": norm2_g, "w_group": w_group,
            "b_group": b_group, "w_router": w_router, "b_router": b_router, "w_gate": w_gate,
            "w_up": w_up, "w_down": w_down, "final_g": final_g}

def second_block(x, c, ctx, c_ctx, w_mod, b_mod, norm1_g, w_in, conv_w, a_log, dt_bias, onorm_g, w_out,
              norm2_g, w_group, b_group, w_router, b_router, w_gate, w_up, w_down, final_g):
    for l in range(DEPTH):
        x, ctx = trunk_layer(x, ctx, c, c_ctx, w_mod[l], b_mod[l], norm1_g[l], w_in[l], conv_w[l], a_log[l],
                             dt_bias[l], onorm_g[l], w_out[l], norm2_g[l], w_group[l], b_group[l],
                             w_router[l], b_router[l], w_gate[l], w_up[l], w_down[l],
                             update_ctx=(l < DEPTH - 1))
    return rmsnorm(x, final_g)


def setup_inputs(seed=0):
    out = dict(first_inputs(seed))
    for name, value in second_inputs(seed + 1).items():
        if name != "x":
            out[name + "_2"] = value
    return out


def reference(
    x, norm1_g, w_in, q_norm_g, k_norm_g, lru_conv_w, lru_conv_b, lru_wa, lru_ba, lru_wx,
    lru_bx, lru_lambda, conf_dw_w, conf_dw_b, conf_ln_g, conf_ln_b, conf_pw_w, conf_pw_b,
    out_norm_g, w_out, norm2_g, router_coarse, router_fine, exp_w_gate, exp_w_up, exp_w_down,
    c_2, ctx_2, c_ctx_2, w_mod_2, b_mod_2, norm1_g_2, w_in_2, conv_w_2, a_log_2, dt_bias_2,
    onorm_g_2, w_out_2, norm2_g_2, w_group_2, b_group_2, w_router_2, b_router_2, w_gate_2,
    w_up_2, w_down_2, final_g_2,
):
    x = first_block(
        x, norm1_g, w_in, q_norm_g, k_norm_g, lru_conv_w, lru_conv_b, lru_wa, lru_ba, lru_wx,
        lru_bx, lru_lambda, conf_dw_w, conf_dw_b, conf_ln_g, conf_ln_b, conf_pw_w, conf_pw_b,
        out_norm_g, w_out, norm2_g, router_coarse, router_fine, exp_w_gate, exp_w_up,
        exp_w_down,
    )
    return second_block(
        x, c_2, ctx_2, c_ctx_2, w_mod_2, b_mod_2, norm1_g_2, w_in_2, conv_w_2, a_log_2,
        dt_bias_2, onorm_g_2, w_out_2, norm2_g_2, w_group_2, b_group_2, w_router_2, b_router_2,
        w_gate_2, w_up_2, w_down_2, final_g_2,
    )


_drawn_inputs = setup_inputs


def setup_inputs(seed=0):
    import zlib

    import numpy as np

    out = dict(_drawn_inputs(seed))
    spreads = {}
    factors = {'lru_ba': 8.0,
     'lru_bx': 6.032,
     'conf_ln_b': 3.786,
     'conf_pw_b': 2.976,
     'ctx_2': 8.0,
     'c_ctx_2': 8.0,
     'b_mod_2': 6.599,
     'norm1_g_2': 8.0,
     'onorm_g_2': 8.0,
     'norm2_g_2': 8.0,
     'b_group_2': 8.0,
     'b_router_2': 8.0,
     'final_g_2': 2.84}
    for name, (base, spread) in spreads.items():
        noise = np.random.default_rng([zlib.crc32(name.encode()), seed]).standard_normal(out[name].shape)
        drawn = base * np.exp(spread * noise) if base else spread * noise
        out[name] = jnp.asarray(drawn.astype(out[name].dtype))
    for name, factor in factors.items():
        out[name] = (out[name] * factor).astype(out[name].dtype)
    return out
```

```python
from contextlib import ExitStack

import concourse.bass as bass
from concourse import mybir

ALU = mybir.AluOpType
ACT = mybir.ActivationFunctionType
F32 = mybir.dt.float32
I32 = mybir.dt.int32
U32 = mybir.dt.uint32
AX = mybir.AxisListType.X

P = 128
T = 512
D = 1024
KD = D // P
TT = T // P
HD = 64
NH = 8
CTX = 256
TC = CTX // P
NE = 32
NG = 4
EG = NE // NG
DE = 512
CAP = 64
NOV = 2 * T // CAP - 1
NBLK = NE + NOV
NSLOT = NBLK * CAP
EPS = 1e-6
CW = 4
FW = 31
UNIT = 4096
RING = 6
NR = NG + NE

PARAMS = [
    ("g1", KD), ("gq", 1), ("gk", 1), ("lcw", 2 * CW), ("lcb", 2), ("lba", 2), ("lbx", 2), ("lam", 2),
    ("dww", 2 * FW), ("dwb", 2), ("lng", 2), ("lnb", 2), ("pwb", 2), ("gout", KD),
    ("g2n", KD), ("g2p", KD), ("h1n", KD), ("h2n", KD), ("h2p", KD), ("onorm", 1),
    ("cvec", 2 * KD), ("cw2", 12 * 9), ("rbias", NR), ("dtb", 8), ("alog", 8),
    ("io32", NE), ("base0", NE), ("base1", NE), ("io4", NG), ("io15", NOV), ("bmc", 8 * KD), ("tokf", TT),
    ("io64", CAP), ("slot0", NBLK + 1),
]
PCOL = {}
NPAR = 0
for _name, _width in PARAMS:
    PCOL[_name] = (NPAR, _width)
    NPAR += _width
MATS = ["ident", "ones", "lt", "le", "ge", "gtd", "ltd", "gtl", "ltl", "blk", "nge", "nones"]


class Banks:

    def __init__(self, banks, full, free):
        self.banks, self.full, self.free, self.names = banks, full, free, []

    def deal(self, pe, name):
        n = len(self.names)
        if n >= len(self.banks):
            pe.wait_ge(self.free, n - len(self.banks) + 1)
        self.names.append(name)
        return self.banks[n % len(self.banks)]

    def at(self, name):
        return self.names.index(name) + 1

    def bank(self, name):
        return self.banks[self.names.index(name) % len(self.banks)]


def build(nc, a, out):
    with ExitStack() as ctx:
        def sb(name, shape, dt=F32):
            return ctx.enter_context(nc.sbuf_tensor(name, shape, dt))

        sems = {}

        def S(name):
            if name not in sems:
                sems[name] = ctx.enter_context(nc.semaphore(name))
            return sems[name]

        def dram(name, shape, dt=F32):
            return nc.dram_tensor(name, shape, dt, kind="Internal").ap()

        ring = sb("ring", [P, RING * UNIT])
        arena = sb("arena", [P, 6 * UNIT])
        par = sb("par", [P, NPAR])
        mats = sb("mats", [P, len(MATS), P])
        rw = sb("rw", [P, 2, KD, NR])
        gw = sb("gw", [P, KD, 16])
        smallf = sb("smallf", [P, 740])
        smalli = sb("smalli", [P, 128], I32)
        psum = [ctx.enter_context(nc.psum_tensor(f"bank{i}", [P, 512], F32)) for i in range(8)]

        modd = dram("modd", (2, 6 * D))
        xnd = [dram(f"xnd{m}", (T, D)) for m in range(2)]
        yd = [dram(f"yd{m}", (NSLOT, D)) for m in range(2)]
        x2d = dram("x2d", (T, D))

        M = {n: mats[:, i, :] for i, n in enumerate(MATS)}

        def pcol(name, j=0, w=1):
            c = PCOL[name][0] + j
            return par[:, c:c + w]

        def area(slot, at, n):
            o = slot * UNIT + at
            return arena[:, o:o + n]

        def chunks(ap, w):
            return ap.rearrange("p (c n) -> p c n", n=w)

        def bc(ap, axis, shape):
            return ap.unsqueeze(axis).to_broadcast(shape)

        taken = [0]

        def small(n):
            o = taken[0]
            taken[0] += n
            assert taken[0] <= 740
            return smallf[:, o:o + n]

        eps, one, gq8, lam8, lamt = small(1), small(1), small(1), small(2), small(4)
        ssq, rstd, cs = small(4), small(4), small(2 * KD)
        mAn, mBn, mAp, mBp = small(KD), small(KD), small(KD), small(KD)
        aX, aC = small(KD), small(KD)
        mc = chunks(small(8 * KD), KD)
        MC = ["x0", "x1", "x3", "x4", "x3p", "x4p", "c0", "c1"]
        gt = chunks(small(6 * 16), 16)
        beta, gval, gcum, gtot, kbs, kds, egl = (chunks(small(48), 8) for _ in range(7))
        nega = small(8)
        w12 = small(8)
        sl = smalli[:, 0:8]
        slots_tok = smalli[0:CAP, 12:12 + NBLK]
        slots_any = smalli[0:CAP, 12:13 + NBLK]
        stage = smalli[0:CAP, 60:62]
        ovt = smalli[0:1, 62:62 + NOV + 1]
        idx8 = chunks(smalli[:, 80:112].bitcast(U32), 8)

        V = Banks(psum[0:4], S("full_v"), S("free_v"))
        C = Banks(psum[4:8], S("full_s"), S("free_s"))

        def cols(w, n):
            return w.rearrange("(c p) n -> p c n", p=P)[:, :, 512 * n:512 * n + 512]

        plain = {}
        U_IN, U_MOD, U_OUT = [1, 5, 10, 15, 16], [0, 2, 3, 4, 6, 7, 8, 9, 11, 12, 13, 14], 17
        for n, u in enumerate(U_MOD):
            plain[u] = cols(a["w_mod"], n)
        for n, u in enumerate(U_IN):
            plain[u] = cols(a["w_in"], n)
        for n in range(2):
            plain[U_OUT + n] = cols(a["w_out"], n)
        U_MOE = [19, 0]
        U_F = U_MOE[0] + 3 * NE
        second = [cols(a["w_in_2"], 0), a["dft"].rearrange("(c p) n -> p c n", p=P)]
        second += [cols(a["w_in_2"], n) for n in range(1, 5)]
        second += [None, None, None] + [cols(a["w_out_2"], n) for n in range(2)]
        U_TILES, U_OUT2 = U_F + 6, U_F + 9
        for n, v in enumerate(second):
            plain[U_F + n] = v
        U_MOE[1] = U_F + len(second)
        used_by = {}

        def unit(u, rows=KD):
            s = u % RING
            return ring[:, s * UNIT:(s + 1) * UNIT].rearrange("p (c n) -> p c n", c=rows)

        def landed(u):
            return S(f"weights{u % RING}"), 16 * (u // RING + 1)

        def freed_expert(m, off):
            if off < 2:
                return S("gu_done"), NE * m + 1
            if off == 3 * NE - 1:
                return S("y_done"), NE * m + NE
            e, j = 1 + (off - 2) // 3, (off - 2) % 3
            return (S("gu_done"), NE * m + e + 1) if j < 2 else (S("y_done"), NE * m + e)

        for m in range(2):
            for off in range(3 * NE):
                used_by[U_MOE[m] + off] = freed_expert(m, off)

        xT = chunks(area(0, 0, 4096), T)
        modv = area(3, 1040, 12 * P)
        qk = chunks(area(1, 0, 4096), T)
        vtok = chunks(area(2, 0, 2048), T)
        upad = chunks(area(2, 2048, 2 * (T + FW - 1)), T + FW - 1)
        pw = chunks(area(2, 3200, 512), 256)
        xrp = chunks(area(3, 0, 2 * (T + CW - 1)), T + CW - 1)
        xge = chunks(area(3, 1040, 1024), T)
        gsig = chunks(area(3, 2064, 1024), T)
        lbd = chunks(area(3, 3088, 512), P)
        sq8 = chunks(area(4, 0, 4096), T)
        root = chunks(area(5, 0, 2048), T)
        sq2 = chunks(area(5, 2048, 1024), T)
        lnx = chunks(area(5, 3072, 1024), T)
        zeros = area(5, 3072, D)
        yT = chunks(area(0, 0, 4096), T)
        xconv, dwo = yT[:, 4:6, :], yT[:, 6:8, :]
        KOFF, KBANK = [0, 512, 1024, 896], [(0, 0), (1, 0), (2, 0), (1, 384)]
        lnb = area(4, 0, 1280)
        spb = [area(4, 1280 + 1280 * i, 1280) for i in range(2)]
        wb = [area(5, 1280 * i, 1280) for i in range(2)]
        zbanks = [psum[0:3], psum[3:6]]

        def kpart(buf, c):
            return buf[:, KOFF[c]:KOFF[c] + T - P * c]

        def zpart(banks, c):
            b, o = KBANK[c]
            return banks[b][:, o:o + T - P * c]

        lr, li, lt_, la = (chunks(area(4, 1024 * i, 1024), T) for i in range(4))
        ld = chunks(area(5, 0, 1024), T)

        x_tok = chunks(area(1, 0, 4096), D)
        xn_tok = chunks(area(2, 0, 4096), D)
        hT3 = chunks(area(3, 0, 4096), T)
        xg = [area(4, 1024 * i, 1024)[0:CAP] for i in range(2)]
        xTs = [area(4, 2048 + 512 * i, 512) for i in range(2)]
        hb = [area(4, 3072 + 512 * i, 512)[0:CAP] for i in range(2)]
        sg = [area(5, 512 * i, 512) for i in range(2)]
        hTs = [area(5, 1024 + 256 * i, 256) for i in range(2)]
        ys = [area(5, 1536 + 512 * i, 512) for i in range(2)]
        GU, XT, Y, HT = psum[0:2], psum[2:4], psum[4:6], psum[6:8]
        rt = [2560]

        def route(n, w=None):
            o = rt[0]
            rt[0] += n
            assert rt[0] <= 4096
            ap = area(5, o, n)
            return chunks(ap, w) if w else ap

        lg = route(TT * NR, NR)
        t16, oh, ex = route(16, NG), route(16, NG), route(16, NG)
        cm, mn, gi, wg = route(4), route(4), route(4), route(4)
        fs, v8, eidf, eid = route(32, EG), route(32, 8), route(8, 2), route(8, 2)
        m1, m2, pick, rk, sm = (route(TT * NE, NE) for _ in range(5))
        cnt, nov, ove, b1 = route(NE), route(NE), route(NE), route(NE)
        dv, ev, den, s12 = route(4), route(4), route(4), route(8)
        ovf = route(16)
        fm = area(4, 0, NE * TT).rearrange("p (t g e) -> p t g e", t=TT, g=NG)
        at_block = chunks(area(4, 1024, 2 * TT * (NBLK + 1)), NBLK + 1)
        in_block = chunks(area(4, 1536, 2 * TT * NBLK), NBLK)
        in_place = chunks(area(4, 2048, 2 * TT * CAP), CAP)
        place = route(2 * TT)
        logitsT = area(4, 3072, T)
        ovc = area(4, 512, NOV * NE)[0:1].rearrange("p (i e) -> p i e", e=NE)
        yg = [[area(2, 2048 * i + 1024 * k, 1024) for k in range(2)] for i in range(2)]
        m5row, fgrow, b5row = area(3, 0, D), area(3, D, D), area(4, 0, D)
        fin = [area(3, 2048 + D * i, D) for i in range(2)]

        hT0 = chunks(area(0, 0, 4096), T)
        hTc = chunks(area(5, 2048, 2048), CTX)
        csq = chunks(area(4, 0, 2048), CTX)
        croot = area(4, 2048, CTX)
        csc = area(5, 0, 256)
        fT = chunks(area(3, 0, 2048), T)
        AB = area(1, 0, 4096).rearrange("p (s g n) -> p s g n", s=TT, g=4)
        y2T = chunks(area(2, 0, 4096), T)
        pad2 = [area(5, 660 * i, 660).rearrange("p (r c) -> p r c", c=66) for i in range(2)]
        padc = [area(5, 1320 + 258 * i, 258) for i in range(2)]
        co = [area(1, 3072 + 512 * i, 512) for i in range(2)]
        coc = [area(2, 2048 + 256 * i, 256) for i in range(2)]
        sqn = area(2, 2560, 512)
        sqc = area(2, 3072, 256)
        rootn = area(2, 3328, 512)
        rootc = area(2, 3840, 256)
        Ktok = area(3, 0, 2048).rearrange("p (t h n) -> p t h n", t=TT, h=4)
        Vtok = area(3, 2048, 2048).rearrange("p (t h n) -> p t h n", t=TT, h=4)
        q2 = chunks(area(4, 0, 2048), T)
        k2 = chunks(area(4, 2048, 2048), T)
        kc = chunks(area(1, 0, 1024), CTX)
        Kc = area(1, 1024, 1024).rearrange("p (t h n) -> p t h n", t=TC, h=4)
        Vc = area(1, 2048, 1024).rearrange("p (t h n) -> p t h n", t=TC, h=4)
        zT = chunks(ring[:, (U_TILES + 2) % RING * UNIT:][:, 0:2048], T)
        Z = [[area(0, 512 * i, 512) for i in range(8)] + [area(5, 2048 + 512 * i, 512) for i in range(4)],
             [ring[:, U_TILES % RING * UNIT + 512 * i:][:, 0:512] for i in range(8)]
             + [ring[:, (U_TILES + 1) % RING * UNIT + 512 * i:][:, 0:512] for i in range(4)]]
        St = [area(1, 3072 + 512 * d, 512) for d in range(2)]
        gatesT = area(3, 2048, CTX + T)
        g2row, b2row = area(3, 0, D), area(3, 2 * D, D)
        mixt = [area(3, D + 512 * i, 512) for i in range(2)]

        def heads(ap):
            return ap.rearrange("p (h n) -> p h n", h=4)

        def hd(ap, h):
            return ap[:, P * h:P * h + P]

        pairs = [(True, (n, TC - 1 - n)) for n in range(TC)] + [(False, (n, TT - 1 - n)) for n in range(TT)]
        LAST = 2 * len(pairs) - 1

        def positive(eng, sem, val):
            if not isinstance(val, int) or val > 0:
                eng.wait_ge(sem, val)

        def settle(eng, sem, val):
            if isinstance(val, int):
                if val > 0:
                    eng.wait_ge(sem, val)
            else:
                eng.wait_ge(sem, val)
                eng.sem_inc(S(f"passed_{eng.engine.name}"), 1)

        block = ctx.enter_context(nc.Block())

        @block.tensor
        def _(pe):
            def use(u):
                pe.wait_ge(*landed(u))
                return unit(u)

            def used(u, banks, name):
                used_by[u] = (banks.full, banks.at(name))

            def colsum(banks, name, mat, tiles, ready, val, n=T):
                b = banks.deal(pe, name)
                pe.wait_ge(S(ready), val)
                for i, t in enumerate(tiles):
                    mm = pe.matmul(b[:, 0:n], mat, t, start=(i == 0), stop=(i == len(tiles) - 1))
                mm.then_inc(banks.full, 1)

            def feature(banks, name, w, col, ap, n=T):
                b = banks.deal(pe, name)
                for k in range(KD):
                    mm = pe.matmul(b[:, 0:n], w[:, k, col:col + P], ap[:, k, :],
                                   start=(k == 0), stop=(k == KD - 1))
                mm.then_inc(banks.full, 1)

            def thin(name, n, w, sources, buf):
                for i, (h, size) in enumerate(sources):
                    b = V.deal(pe, f"{name}T{i}")
                    for k in range(KD):
                        r = 64 * (k % 2)
                        mm = pe.matmul(b[r:r + n, 0:size], w[:, k, :], h[:, k, :], start=(k < 2), stop=(k >= KD - 2),
                                       skip_group_check=True)
                    mm.then_inc(V.full, 1)
                b = V.deal(pe, name)
                pe.wait_ge(V.free, V.at(f"{name}T{len(sources) - 1}"))
                for t in range(sum(size for _, size in sources) // P):
                    mm = pe.matmul(b[:, n * t:n * t + n], buf[0:n, P * t:P * t + P], M["ident"][0:n, 0:n],
                                   start=True, stop=True)
                mm.then_inc(V.full, 1)

            pe.wait_ge(S("params"), 16 * 2)
            def modulation(n0, n1):
                for n in range(n0, n1):
                    w = use(U_MOD[n])
                    b = V.deal(pe, f"mod{n}")
                    for k in range(KD):
                        for g in range(4):
                            mm = pe.matmul(b[32 * g:32 * g + 2, 0:P], chunks(cs, 2)[:, k, :], w[:, k, P * g:P * g + P],
                                           start=(k == 0), stop=(k == KD - 1), skip_group_check=True)
                    mm.then_inc(V.full, 1)
                    used(U_MOD[n], V, f"mod{n}")

            pe.wait_ge(S("silu_c"), 1)
            modulation(0, 1)
            colsum(C, "ss_x", M["ones"], [sq8[:, k, :] for k in range(KD)], "sq_x", KD)
            pe.wait_ge(S("h_ready"), KD)
            for n in range(8):
                if n == 4:
                    modulation(1, 4)
                w = use(U_IN[n // 4])
                feature(V, f"qk{n}", w, P * (n % 4), xT)
                if n:
                    colsum(C, f"ss_qk{n - 1}", M["blk"], [sq2[:, (n - 1) % 2, :]], "sq_qk", n)
                used(U_IN[n // 4], V, f"qk{n}")
            modulation(4, 8)
            w = use(U_IN[2])
            for s in range(TT):
                b = C.deal(pe, f"v{s}")
                for k in range(KD):
                    mm = pe.matmul(b[:, :], xT[:, k, P * s:P * s + P], w[:, k, :],
                                   start=(k == 0), stop=(k == KD - 1))
                mm.then_inc(C.full, 1)
                if s == 0:
                    colsum(C, "ss_qk7", M["blk"], [sq2[:, 1, :]], "sq_qk", 8)
            used(U_IN[2], C, f"v{TT - 1}")
            modulation(8, 12)
            w = use(U_IN[3])
            for c in range(2):
                feature(V, f"xr{c}", w, P * c, xT)
                feature(C, f"xg{c}", w, 256 + P * c, xT)
            used(U_IN[3], C, "xg1")
            w = use(U_IN[4])
            for c in range(2):
                feature(C, f"cg{c}", w, 256 + P * c, xT)
                feature(V, f"cv{c}", w, P * c, xT)
            used(U_IN[4], V, "cv1")

            pe.wait_ge(V.free, len(V.names))
            pe.wait_ge(C.free, len(C.names))
            pe.wait_ge(S("qk_ready"), 8)

            def scores(h):
                z = zbanks[h % 2]
                if h >= 2:
                    pe.wait_ge(S("w_raw"), 3 * (h - 1))
                r = HD * (h % 2)
                for c in (0, 1, 3, 2):
                    mm = pe.matmul(zpart(z, c), qk[r:r + HD, 4 + h // 2, P * c:P * c + P],
                                   qk[r:r + HD, h // 2, P * c:T], start=(c != 3), stop=True,
                                   skip_group_check=True)
                mm.then_inc(S("z_ready"), 1)

            def decays(h):
                z = zbanks[h % 2]
                pe.wait_ge(S("sp_ready"), h + 1)
                for c in range(4):
                    for c2 in range(c, 4):
                        mm = pe.matmul(zpart(z, c)[:, P * (c2 - c):], M["nge"] if c2 == c else M["nones"],
                                       kpart(spb[h % 2], c2), start=False, stop=(c2 == 3),
                                       skip_group_check=True)
                mm.then_inc(S("arg_ready"), 1)

            def values(h):
                o = psum[6 + (h // 2) % 2]
                r = HD * (h % 2)
                pe.wait_ge(S("w_ready"), h + 1)
                if h >= 4 and h % 2 == 0:
                    pe.wait_ge(S("o_taken"), h // 2 - 1)
                for c in range(4):
                    mm = pe.matmul(o[r:r + HD, P * c:T], vtok[:, c, HD * h:HD * h + HD], kpart(wb[h % 2], c),
                                   start=(c == 0), stop=(c == 3), skip_group_check=True)
                mm.then_inc(S("o_ready"), 1)

            scores(0)
            for h in range(NH):
                if h + 1 < NH:
                    scores(h + 1)
                if h:
                    values(h - 1)
                decays(h)
            values(NH - 1)
            pe.wait_ge(S("o_taken"), NH // 2)
            pe.wait_ge(S("w_raw"), 3 * NH)

            colsum(V, "mu", M["ones"], [dwo[:, c, :] for c in range(2)], "dwconv", 2)
            pe.wait_ge(S("xconv"), 2)
            pe.wait_ge(S("parts1"), 16 * 4)
            for c in range(2):
                for g in range(2):
                    b = C.deal(pe, f"lru{c}{g}")
                    pe.matmul(b[:, :], lbd[:, 2 * g + c, :], xconv[:, c, :], start=True, stop=True)\
                      .then_inc(C.full, 1)
            colsum(C, "ss_ln", M["ones"], [sq2[:, c, :] for c in range(2)], "sq_ln", 2)
            pe.wait_ge(S("ln_silu"), 2)
            for e in range(2):
                b = C.deal(pe, f"pw{e}")
                for c in range(2):
                    mm = pe.matmul(b[:, :], pw[:, c, P * e:P * e + P], lnx[:, c, :], start=(c == 0), stop=(c == 1))
                mm.then_inc(C.full, 1)
            for name, k0, k1 in (("ss_a", 0, 4), ("ss_b", 4, 6), ("ss_c", 6, 8)):
                colsum(C, name, M["ones"], [sq8[:, k, :] for k in range(k0, k1)], "sq_y", k1)

            def project(u, tag, yt, ready):
                for n in range(2):
                    w = use(u + n)
                    banks = [V.deal(pe, f"{tag}{n}{t}") for t in range(TT)]
                    for k0, k1, val in ready if n == 0 else [(0, KD, 0)]:
                        if val:
                            pe.wait_ge(S(f"{tag}_ready"), val)
                        for t in range(TT):
                            for k in range(k0, k1):
                                mm = pe.matmul(banks[t][:, :], yt[:, k, P * t:P * t + P], w[:, k, :],
                                               start=(k == 0), stop=(k == KD - 1), skip_group_check=True)
                            if k1 == KD:
                                mm.then_inc(V.full, 1)
                    used(u + n, V, f"{tag}{n}{TT - 1}")

            project(U_OUT, "outA", yT, [(0, 4, 4), (4, 6, 6), (6, 8, 8)])

            def turn(tag, ready):
                pe.wait_ge(S(ready), TT)
                for k in range(KD):
                    b = C.deal(pe, f"{tag}{k}")
                    for t in range(TT):
                        mm = pe.transpose(b[:, P * t:P * t + P], xn_tok[:, t, P * k:P * k + P], M["ident"])
                    mm.then_inc(C.full, 1)

            def experts(m):
                def turn_x(e, u, ready_val):
                    settle(pe, S(f"gathered{u}"), ready_val)
                    for c in range(KD):
                        mm = pe.transpose(XT[u][:, CAP * c:CAP * c + CAP], xg[u][:, c::KD], M["ident"][0:CAP, 0:CAP])
                    mm.then_inc(S("xt_done"), 1)

                def gate_up(u, wg_, wu_):
                    for c in range(KD):
                        x = xTs[u][:, CAP * c:CAP * c + CAP]
                        pe.matmul(GU[u][0:CAP, :], x, wg_[:, c, :], start=(c == 0), stop=(c == KD - 1),
                                  skip_group_check=True)
                        mm = pe.matmul(GU[u][CAP:2 * CAP, :], x, wu_[:, c, :], start=(c == 0), stop=(c == KD - 1),
                                       skip_group_check=True)
                    mm.then_inc(S("gu_done"), 1)

                def down(u, wd_):
                    for c in range(4):
                        x = hTs[u][:, CAP * c:CAP * c + CAP]
                        pe.matmul(Y[u][0:CAP, :], x, wd_[:, c, 0:512], start=(c == 0), stop=(c == 3),
                                  skip_group_check=True)
                        mm = pe.matmul(Y[u][CAP:2 * CAP, :], x, wd_[:, c, 512:1024], start=(c == 0), stop=(c == 3),
                                       skip_group_check=True)
                    mm.then_inc(S("y_done"), 1)

                def turn_h(u):
                    for c in range(4):
                        mm = pe.transpose(HT[u][:, CAP * c:CAP * c + CAP], hb[u][:, c::4], M["ident"][0:CAP, 0:CAP])
                    mm.then_inc(S("ht_done"), 1)

                def step(e, q, i=None, last=False):
                    n = NE * m + e

                    def weights(off0, j):
                        k = U_MOE[m] + off0 + j
                        settle(pe, S(f"weights{k % RING}"), 16 * (k // RING + 1) if i is None else 16 * (i + (k // RING + 1)))
                        return unit(k, KD if j < 2 else 4)

                    off0 = (3 * e - 1 if i is None else 5 + 3 * q) if i is not None or e else 0
                    settle(pe, S("xs_ready"), n + 1)
                    settle(pe, S("h_done"), n - 1)
                    wg_, wu_ = weights(off0, 0), weights(off0, 1)
                    gate_up(q, wg_, wu_)
                    if not last:
                        turn_x(None, 1 - q, 16 * (NE // 2 * m + (e + 1) // 2 + 1) if i is None
                               else 16 * (i + (NE // 2 * m + (3 + q) // 2 + 1)))
                    if i is not None or e:
                        settle(pe, S("hts_ready"), n)
                        settle(pe, S("y_taken"), n - 2)
                        down(1 - q, weights(off0, 2))
                    settle(pe, S("h_done"), n + 1)
                    turn_h(q)

                pe.wait_ge(V.free, len(V.names))
                pe.wait_ge(C.free, len(C.names))
                turn_x(0, 0, 16 * (NE // 2 * m + 1))
                step(0, 0)
                step(1, 1)
                with nc.tensor.Fori(0, NE // 2 - 2) as i:
                    for q in range(2):
                        step(i * 2 + (2 + q), q, i)
                step(NE - 2, 0)
                step(NE - 1, 1, last=True)
                pe.wait_ge(S("hts_ready"), NE * (m + 1))
                k = U_MOE[m] + 3 * NE - 1
                pe.wait_ge(*landed(k))
                down(1, unit(k, 4))
                beyond_y = S(f"beyond_y{m}")
                pe.wait_ge(S("h_done"), NE * (m + 1))
                pe.sem_inc(beyond_y, 1)
                for name in ("y_taken", "h_done", "xs_ready", "hts_ready"):
                    pe.wait_ge(S(name), NE * (m + 1))
                pe.sem_inc(beyond_y, 1)
                baton = S(f"beyond{m}")
                pe.wait_ge(S("routed"), m + 1)
                n_over = pe.value_load(ovt[0:1, NOV:NOV + 1], min_val=0, max_val=NOV)
                with nc.tensor.Fori(0, (NOV + 1) // 2) as i:
                    for q in range(2):
                        with pe.If(n_over > i * 2 + q):
                            at = i * 16 + (8 * q + 16)
                            u = U_MOE[m] + 3 * NE + 3 * q
                            wg_, wu_, wd_ = unit(u), unit(u + 1), unit(u + 2, 4)
                            settle(pe, S(f"beyond_x{m}{q}"), (i + 1) * 16)
                            for c in range(KD):
                                mm = pe.transpose(XT[0][:, CAP * c:CAP * c + CAP], xg[q][:, c::KD],
                                                  M["ident"][0:CAP, 0:CAP])
                            mm.then_inc(baton, 1)
                            settle(pe, S(f"beyond_w{m}{q}"), (i + 1) * 48)
                            settle(pe, baton, at + 3)
                            for c in range(KD):
                                x = xTs[0][:, CAP * c:CAP * c + CAP]
                                pe.matmul(GU[0][0:CAP, :], x, wg_[:, c, :], start=(c == 0), stop=(c == KD - 1),
                                          skip_group_check=True)
                                mm = pe.matmul(GU[0][CAP:2 * CAP, :], x, wu_[:, c, :], start=(c == 0),
                                               stop=(c == KD - 1), skip_group_check=True)
                            mm.then_inc(baton, 1)
                            settle(pe, baton, at + 6)
                            for c in range(4):
                                mm = pe.transpose(HT[0][:, CAP * c:CAP * c + CAP], hb[0][:, c::4],
                                                  M["ident"][0:CAP, 0:CAP])
                            mm.then_inc(baton, 1)
                            settle(pe, baton, at + 8)
                            for c in range(4):
                                x = hTs[0][:, CAP * c:CAP * c + CAP]
                                pe.matmul(Y[0][0:CAP, :], x, wd_[:, c, 0:512], start=(c == 0), stop=(c == 3),
                                          skip_group_check=True)
                                mm = pe.matmul(Y[0][CAP:2 * CAP, :], x, wd_[:, c, 512:1024], start=(c == 0),
                                               stop=(c == 3), skip_group_check=True)
                            mm.then_inc(beyond_y, 1)
                            settle(pe, baton, at + 9)

            def moe(m):
                turn(f"turn{m}_", f"xn{m}")
                pe.wait_ge(C.free, C.at(f"turn{m}_{KD - 1}"))
                thin(f"logits{m}", NR, rw[:, m], [(hT3, T)], logitsT)
                b = V.deal(pe, f"rank{m}")
                pe.wait_ge(S("picked"), m + 1)
                for t in range(TT):
                    for s in range(t + 1):
                        pe.matmul(b[:, NE * t:NE * t + NE], M["lt"] if s == t else M["ones"], pick[:, s, :],
                                  start=(s == 0), stop=(s == t))
                for s in range(TT):
                    mm = pe.matmul(b[:, NE * TT:NE * TT + NE], M["ones"], pick[:, s, :],
                                   start=(s == 0), stop=(s == TT - 1))
                mm.then_inc(V.full, 1)
                b = V.deal(pe, f"slots{m}")
                pe.wait_ge(S("placed"), m + 1)
                for c in range(2 * TT):
                    mm = pe.matmul(b[0:CAP, 0:NBLK], in_place[:, c, :], in_block[:, c, :],
                                   start=(c == 0), stop=(c == 2 * TT - 1))
                mm.then_inc(V.full, 1)
                experts(m)

            moe(0)

            colsum(C, "ss_ctx", M["ones"], [csq[:, k, :] for k in range(KD)], "sq_ctx", KD, n=CTX)
            turn("turnX", "xn2")
            pe.wait_ge(C.free, C.at(f"turnX{KD - 1}"))
            w = use(U_F)
            for g in range(4):
                feature(C, f"f{g}", w, P * g, hT0)
            used(U_F, C, "f3")
            pe.wait_ge(C.free, C.at("f3"))
            pe.wait_ge(S("parts2"), 16)
            for s in range(TT):
                for gp in range(2):
                    banks = V if gp == 0 else C
                    b = banks.deal(pe, f"ab{s}{gp}")
                    for g in range(2):
                        mm = pe.matmul(b[:, 256 * g:256 * g + 256], fT[:, 2 * gp + g, P * s:P * s + P], csc,
                                       start=True, stop=True)
                    mm.then_inc(banks.full, 1)
            pe.wait_ge(V.free, V.at(f"ab{TT - 1}0"))
            pe.wait_ge(C.free, C.at(f"ab{TT - 1}1"))
            w = use(U_F + 1)
            for g in range(4):
                b = V.deal(pe, f"dft{g}")
                for s in range(TT):
                    pe.matmul(b[:, :], AB[:, s, g, 0:P], w[:, s, :], start=(s == 0), stop=False)
                    mm = pe.matmul(b[:, :], AB[:, s, g, P:2 * P], w[:, TT + s, :], start=False, stop=(s == TT - 1))
                mm.then_inc(V.full, 1)
            used(U_F + 1, V, "dft3")

            pe.wait_ge(S("ctx_ready"), KD)

            def log_decays():
                b = V.deal(pe, "cums")
                pe.wait_ge(S("gval"), 1)
                for t in range(6):
                    pe.matmul(b[:, 8 * t:8 * t + 4], M["le"], gval[:, t, 0:4], start=True, stop=True)
                    pe.matmul(b[:, 8 * t + 4:8 * t + 8], M["ge"], gval[:, t, 4:8], start=True, stop=True)
                    mm = pe.matmul(b[:, 48 + 8 * t:56 + 8 * t], M["ones"], gval[:, t, :], start=True, stop=True)
                mm.then_inc(V.full, 1)

            def norm_sum(n):
                colsum(C, f"ssx{n}", M["ones"], [sqn], "sq2x", n + 1)
                if n >= 4:
                    colsum(C, f"ssc{n}", M["ones"], [sqc], "sq2c", n - 3, n=CTX)

            def turn_kv(n):
                if n < 8:
                    pe.wait_ge(S("norm2x"), n + 1)
                    pe.wait_ge(S("norm2c"), n - 3)
                    src, srcc = k2[:, n - 4, :], kc[:, n - 4, :]
                else:
                    pe.wait_ge(S("vx"), n - 7)
                    pe.wait_ge(S("vc"), n - 7)
                    src, srcc = co[n % 2], coc[n % 2]
                b = C.deal(pe, f"tx{n}")
                for t in range(TT):
                    mm = pe.transpose(b[:, P * t:P * t + P], src[:, P * t:P * t + P], M["ident"])
                mm.then_inc(C.full, 1)
                b = C.deal(pe, f"tc{n}")
                for t in range(TC):
                    mm = pe.transpose(b[:, P * t:P * t + P], srcc[:, P * t:P * t + P], M["ident"])
                mm.then_inc(C.full, 1)

            thin("gates", 16, gw, [(hTc, CTX), (hT0, T)], gatesT)
            for n in range(14):
                if n == 1:
                    log_decays()
                if n < 12:
                    w = use(U_F + 2 + n // 4)
                    feature(V, f"px{n}", w, P * (n % 4), hT0)
                    if n >= 4:
                        feature(V, f"pc{n}", w, P * (n % 4), hTc, n=CTX)
                    used(U_F + 2 + n // 4, V, f"pc{n}" if n >= 4 else f"px{n}")
                if n in (4, 6, 8, 10):
                    feature(C, f"z{n // 2 - 2}", use(U_F + 5), P * (n // 2 - 2), hT0)
                if 1 <= n <= 8:
                    norm_sum(n - 1)
                if n >= 6:
                    turn_kv(n - 2)
            used(U_F + 5, C, "z3")
            pe.wait_ge(C.free, len(C.names))

            def four(banks, name, si, lhs, rhs):
                b = banks.deal(pe, f"{name}{si}")
                for h in range(4):
                    mm = pe.matmul(hd(b, h), lhs(h) if callable(lhs) else hd(lhs, h),
                                   rhs(h) if callable(rhs) else hd(rhs, h), start=True, stop=True)
                mm.then_inc(banks.full, 1)

            def after(banks, name, si):
                pe.wait_ge(banks.free, banks.at(f"{name}{si}"))

            for n, (isc, tiles) in enumerate(pairs):
                kT = kc if isc else k2
                both = [(d, 2 * n + d, Z[d], slice(P * tiles[d], P * tiles[d] + P)) for d in range(2)]
                for d, si, z, tok in both:
                    tau = tiles[d] if isc else TC + tiles[d]
                    four(C, "row", si, lambda h: gval[:, tau, 4 * d + h:4 * d + h + 1].to_broadcast([P, P]),
                         lambda h: M["le"] if d == 0 else M["ge"])
                for d, si, z, tok in both:
                    four(V, "kk", si, lambda h: kT[:, h, tok], lambda h: kT[:, h, tok])
                if not isc:
                    for d, si, z, tok in both:
                        four(V, "kq", si, lambda h: kT[:, h, tok], lambda h: q2[:, h, tok])
                for d, si, z, tok in both:
                    b = V.deal(pe, f"DT{si}")
                    pe.wait_ge(S("dl_ready"), si + 1)
                    for h in range(4):
                        mm = pe.transpose(hd(b, h), hd(z[5], h), M["ident"])
                    mm.then_inc(V.full, 1)
                for d, si, z, tok in both:
                    after(V, "DT", si)
                    four(C, "D2", si, z[0], z[5])
                    four(C, "D2T", si, z[5], z[0])
                for d, si, z, tok in both:
                    after(C, "D2", si)
                    four(V, "F1", si, z[4], z[1])
                    after(C, "D2T", si)
                    four(C, "D4", si, z[9], z[4])
                    four(C, "D4T", si, z[4], z[9])
                for d, si, z, tok in both:
                    after(V, "F1", si)
                    after(C, "D4", si)
                    four(V, "F2", si, z[10], z[1])
                    after(C, "D4T", si)
                    four(C, "D8", si, z[11], z[10])
                for d, si, z, tok in both:
                    after(V, "F2", si)
                    after(C, "D8", si)
                    four(V, "F3", si, z[11], z[1])
                for d, si, z, tok in both:
                    after(V, "F3", si)
                    four(V, "GT", si, z[6], z[1])
                    four(C, "G", si, z[1], z[6])
                for d, si, z, tok in both:
                    pe.wait_ge(S("kv_scaled"), 2 * (si + 1))
                    four(C, "RV", si, z[1], z[7])
                    four(C, "RK", si, z[1], z[8])
                for d, si, z, tok in both:
                    after(V, "GT", si)
                    after(C, "G", si)
                    four(C, "G2", si, z[4], z[0])
                    four(C, "G2T", si, z[0], z[4])
                for d, si, z, tok in both:
                    after(C, "G2", si)
                    four(V, "H1", si, z[10], z[9])
                    after(C, "G2T", si)
                    four(C, "G4", si, z[11], z[10])
                for d, si, z, tok in both:
                    after(V, "H1", si)
                    after(C, "G4", si)
                    four(V, "H2", si, z[11], z[9])
                for d, si, z, tok in both:
                    after(V, "H2", si)
                    four(C, "U", si, z[9], z[7])
                    four(C, "WT", si, z[8], z[9])
                for d, si, z, tok in both:
                    after(C, "WT", si)
                    four(V, "WS", si, z[4], St[d])
                if not isc:
                    for d, si, z, tok in both:
                        after(V, "WS", si)
                        b = V.deal(pe, f"OT{si}")
                        pe.wait_ge(S("qe_scaled"), si - 2 * TC + 1)
                        for h in range(4):
                            pe.matmul(hd(b, h), hd(St[d], h), hd(z[2], h), start=True, stop=False)
                            mm = pe.matmul(hd(b, h), hd(z[6], h), hd(z[3], h), start=False, stop=True)
                        mm.then_inc(V.full, 1)
                for d, si, z, tok in both:
                    after(V, "WS", si)
                    pe.wait_ge(S("kd_scaled"), si + 1)
                    four(V, "SU", si, z[10], z[6])
            for u in (U_TILES, U_TILES + 1):
                used(u, V, f"SU{LAST}")
            used_by[U_TILES + 2] = (S("outB_ready"), 4)

            for h in range(4):
                colsum(C, f"so{h}", M["ones"], [Z[0][h]], "sq_o", h + 1)
            project(U_OUT2, "outB", y2T, [(0, 4, 0), (4, 8, 4)])
            moe(1)

        @block.sync
        def _(sp):
            sp.dma_start(par[:, :], a["par"]).then_inc(S("params"), 16)
            sp.dma_start(mats[:, :, :], a["mats"].rearrange("p (n f) -> p n f", f=P)).then_inc(S("params"), 16)
            sp.dma_start(xT, a["xT"].rearrange("(c p) t -> p c t", p=P)).then_inc(S("x_in"), 16)

            def split_weights(w, chunks_):
                return w.rearrange("e (p c) n -> e p c n", c=chunks_)

            expert_weights = [(split_weights(a["w_gate" + x], KD), split_weights(a["w_up" + x], KD),
                               split_weights(a["w_down" + x], 4)) for x in ("", "_2")]

            def load_e(m, off, e, i=None):
                k = U_MOE[m] + off
                kind = off if off < 2 else 2 if off == 3 * NE - 1 else (off - 2) % 3
                w = expert_weights[m][kind]
                sem, val = used_by[k - RING]
                if i is None:
                    sp.wait_ge(sem, val)
                    src = w[e]
                else:
                    sp.wait_ge(sem, i * 2 + val)
                    src = w[bass.ds(e, 1)].rearrange("e p c n -> (e p) c n")
                sp.dma_start(unit(k, src.shape[1]), src).then_inc(S(f"weights{k % RING}"), 16)

            def load(u):
                if u >= RING:
                    sp.wait_ge(*used_by[u - RING])
                if plain[u] is None:
                    sp.sem_inc(landed(u)[0], 16)
                    return
                rows = plain[u].shape[1]
                sp.dma_start(unit(u, rows), plain[u]).then_inc(landed(u)[0], 16)

            load(0)
            load(1)
            sp.dma_start(lbd, a["lbd"].rearrange("p (c n) -> p c n", c=4)).then_inc(S("parts1"), 16)
            sp.dma_start(rw[:, :, :, :], a["rw"].rearrange("p (m c n) -> p m c n", m=2, c=KD)).then_inc(S("parts1"), 16)
            sp.dma_start(gw[:, :, :], a["gw"].rearrange("p (c n) -> p c n", c=KD)).then_inc(S("parts1"), 16)
            for u in range(2, 17):
                load(u)
            sp.wait_ge(V.free, V.at("mod11"))
            for g in range(4):
                sp.dma_start(modd.rearrange("r (n g j) -> g r n j", n=12, g=4)[g],
                             modv[32 * g:32 * g + 2, :].rearrange("r (n j) -> r n j", n=12)).then_inc(S("mod_out"), 16)
            sp.wait_ge(S("mod_out"), 16 * 4)
            nat = modd.rearrange("r (j c p) -> p r j c", c=KD, p=P)
            perm = modd.rearrange("r (j p c) -> p r j c", c=KD, p=P)
            for i, (v, r, j) in enumerate([(nat, 0, 0), (nat, 0, 1), (nat, 0, 3), (nat, 0, 4),
                                           (perm, 0, 3), (perm, 0, 4), (nat, 1, 0), (nat, 1, 1)]):
                sp.dma_start(mc[:, i, :], v[:, r, j, :], allow_slow_non_contiguous=True).then_inc(S("mod_cols"), 16)
            sp.dma_start(pw, a["pw"].rearrange("(c p) n -> p c n", p=P)).then_inc(S("parts1"), 16)
            sp.wait_ge(S("zeros"), 1)
            for m in range(2):
                sp.dma_start(yd[m][NE * CAP:NSLOT, :].rearrange("(p r) d -> p r d", r=8),
                             zeros[0:NOV * CAP // 8].unsqueeze(1).to_broadcast([NOV * CAP // 8, 8, D]))\
                  .then_inc(S("yd_zero"), 16)
            load(17)
            load(18)
            load_e(0, 0, 0)
            load_e(0, 1, 0)
            load_e(0, 2, 1)
            load_e(0, 3, 1)
            sp.wait_ge(S("z_ready"), NH)
            sp.dma_start(x_tok, a["x"].rearrange("(t p) d -> p t d", p=P)).then_inc(S("x_again"), 16)

            def experts(m):
                load_e(m, 4, 0)
                load_e(m, 5, 2)
                for t in range(TT):
                    sp.wait_ge(S(f"xn{m}"), t + 1)
                    sp.dma_start(xnd[m][P * t:P * t + P, :], xn_tok[:, t, :]).then_inc(S("xn_out"), 16)
                for off in range(6, 11):
                    load_e(m, off, (off + 1) // 3 - (off % 3 == 1))
                with nc.sync.Fori(0, NE // 2 - 2) as i:
                    for q in range(2):
                        off = 3 * (4 + q) - 1
                        load_e(m, off, i * 2 + (4 + q), i)
                        load_e(m, off + 1, i * 2 + (4 + q), i)
                        load_e(m, off + 2, i * 2 + (3 + q), i)
                load_e(m, 3 * NE - 1, NE - 1)
                beyond_y = S(f"beyond_y{m}")
                sp.wait_ge(S("routed"), m + 1)
                n_over = sp.value_load(ovt[0:1, NOV:NOV + 1], min_val=0, max_val=NOV)
                with nc.sync.Fori(0, (NOV + 1) // 2) as i:
                    for q in range(2):
                        with sp.If(n_over > i * 2 + q):
                            settle(sp, beyond_y, i * 2 + (q + 1))
                            e = sp.value_load(ovt[0:1, bass.ds(i * 2 + q, 1)], min_val=0, max_val=NE - 1)
                            for j, w in enumerate(expert_weights[m]):
                                src = w[bass.ds(e, 1)].rearrange("e p c n -> (e p) c n")
                                u = U_MOE[m] + 3 * NE + 3 * q + j
                                sp.dma_start(unit(u, src.shape[1]), src).then_inc(S(f"beyond_w{m}{q}"), 16)
                settle(sp, beyond_y, n_over + 2)

            experts(0)
            for q in range(2):
                sp.wait_ge(S(f"stored{q}"), 32 * (NE // 2))
            sp.wait_ge(S("yd_done"), 1)
            sp.dma_start(hTc, a["ctxT"].rearrange("(c p) t -> p c t", p=P)).then_inc(S("ctx_in"), 16)
            sp.dma_start(csc, a["csc"]).then_inc(S("parts2"), 16)
            sp.wait_ge(S("x2_ready"), TT)
            load(U_F)
            sp.dma_start(x2d.rearrange("(t p) d -> p t d", p=P), x_tok).then_inc(S("x2_out"), 16)
            for u in range(U_F + 1, U_F + len(second)):
                load(u)
            load_e(1, 0, 0)
            sp.wait_ge(V.free, V.at(f"SU{LAST}"))
            sp.wait_ge(S("x2_out"), 16)
            sp.dma_start(x_tok, x2d.rearrange("(t p) d -> p t d", p=P)).then_inc(S("x2_again"), 16)
            sp.dma_start(g2row, modd[0:1, 2 * D:3 * D].partition_broadcast(P)).then_inc(S("x2_again"), 16)
            sp.dma_start(b2row, a["bmod"][:, 2 * D:3 * D].partition_broadcast(P)).then_inc(S("x2_again"), 16)
            load_e(1, 1, 0)
            load_e(1, 2, 1)
            load_e(1, 3, 1)
            experts(1)
            sp.wait_ge(C.free, len(C.names))
            sp.wait_ge(S("y_taken"), 2 * NE)
            sp.dma_start(m5row, modd[0:1, 5 * D:6 * D].partition_broadcast(P)).then_inc(S("rows"), 16)
            sp.dma_start(b5row, a["bmod"][:, 5 * D:6 * D].partition_broadcast(P)).then_inc(S("rows"), 16)
            sp.dma_start(fgrow, a["fg"].partition_broadcast(P)).then_inc(S("rows"), 16)
            for t in range(TT):
                sp.wait_ge(S("out_ready"), t + 1)
                sp.dma_start(out[P * t:P * t + P, :], fin[t % 2]).then_inc(S(f"out{t % 2}"), 16)
            sp.wait_ge(S("out0"), 16 * 2)
            sp.wait_ge(S("out1"), 16 * 2)

        @block.gpsimd
        def _(pool):
            pool.wait_ge(S("params"), 16 * 2)
            for h in range(NH + 1):
                if h < NH:
                    pool.wait_ge(S("sp_raw"), 3 * (h + 1))
                    for c in range(4):
                        d = kpart(spb[h % 2], c)[:, 0:P]
                        last = pool.tensor_tensor(d, d, M["lt"], ALU.mult)
                    last.then_inc(S("sp_ready"), 1)
                if h:
                    pool.wait_ge(S("w_raw"), 3 * h)
                    for c in range(4):
                        d = kpart(wb[(h - 1) % 2], c)[:, 0:P]
                        last = pool.affine_select(out=d, in_=d, pattern=[[1, P]], compare_op=ALU.is_gt,
                                                  fill=0.0, base=0, channel_multiplier=-1)
                    last.then_inc(S("w_ready"), 1)

            def experts(m):
                pool.wait_ge(V.free, V.at(f"slots{m}"))
                pool.wait_ge(S("yd_zero"), 16 * 2)
                pool.wait_ge(S("xn_out"), 16 * TT * (m + 1))

                def gather(e, q):
                    n = NE * m + e
                    settle(pool, S("xt_done"), n - 1)
                    pool.tensor_copy(stage[:, q:q + 1], slots_tok[:, bass.ds(e, 1)]).then_inc(S("staged"), 1)
                    settle(pool, S("staged"), n + 1)
                    pool.indirect_dma_start(
                        out=xg[q], out_offset=None, in_=xnd[m],
                        in_offset=bass.IndirectOffsetOnAxis(ap=stage[:, q:q + 1], axis=0))\
                        .then_inc(S(f"gathered{q}"), 16)

                gather(0, 0)
                gather(1, 1)
                with nc.gpsimd.Fori(0, NE // 2 - 1) as i:
                    for q in range(2):
                        gather(i * 2 + (2 + q), q)
                baton = S(f"beyond{m}")
                n_over = pool.value_load(ovt[0:1, NOV:NOV + 1], min_val=0, max_val=NOV)
                with nc.gpsimd.Fori(0, (NOV + 1) // 2) as i:
                    for q in range(2):
                        with pool.If(n_over > i * 2 + q):
                            pool.wait_ge(S("xt_done"), NE * (m + 1))
                            settle(pool, baton, i * 16 + (8 * q + 2))
                            pool.tensor_copy(stage[:, q:q + 1], slots_any[:, bass.ds(i * 2 + (NE + q), 1)])\
                                .then_inc(S(f"beyond_s{m}"), 1)
                            settle(pool, S(f"beyond_s{m}"), i * 2 + (q + 1))
                            pool.indirect_dma_start(
                                out=xg[q], out_offset=None, in_=xnd[m],
                                in_offset=bass.IndirectOffsetOnAxis(ap=stage[:, q:q + 1], axis=0))\
                                .then_inc(S(f"beyond_x{m}{q}"), 16)
                settle(pool, S(f"beyond_st{m}"), n_over * 32 + 32)
                for q in range(2):
                    pool.wait_ge(S(f"stored{q}"), 32 * (NE // 2) * (m + 1))
                pool.sem_inc(S("yd_done"), 1)
                for t in range(TT):
                    if t >= 2:
                        pool.wait_ge(S(f"combined{m}"), t - 1)
                    for k in range(2):
                        c = TT * k + t
                        pool.indirect_dma_start(
                            out=yg[t % 2][k], out_offset=None, in_=yd[m],
                            in_offset=bass.IndirectOffsetOnAxis(ap=sl[:, c:c + 1], axis=0))\
                            .then_inc(S(f"y_in{t % 2}"), 16)

            experts(0)
            for n, (isc, tiles) in enumerate(pairs):
                K_, V_ = (Kc, Vc) if isc else (Ktok, Vtok)

                def scaled(col, d):
                    tau = tiles[d] if isc else TC + tiles[d]
                    return bc(col[:, tau, 4 * d:4 * d + 4], 2, [P, 4, P])

                for d in range(2):
                    if n == 0:
                        pool.wait_ge(S("cols2"), 1)
                        pool.wait_ge(C.free, C.at("tc11"))
                    else:
                        pool.wait_ge(V.full, V.at(f"SU{2 * n - 2 + d}"))
                    pool.tensor_tensor(heads(Z[d][7]), V_[:, tiles[d]], scaled(beta, d), ALU.mult)\
                        .then_inc(S("kv_scaled"), 1)
                    pool.tensor_tensor(heads(Z[d][8]), K_[:, tiles[d]], scaled(kbs, d), ALU.mult)\
                        .then_inc(S("kv_scaled"), 1)
                if not isc:
                    for d in range(2):
                        pool.wait_ge(S("rows_exp"), 2 * (n - TC) + d + 1)
                        q_ = q2[:, :, P * tiles[d]:P * tiles[d] + P]
                        pool.tensor_tensor(heads(Z[d][2]), heads(Z[d][2]), q_, ALU.mult).then_inc(S("qe_scaled"), 1)
                for d in range(2):
                    pool.wait_ge(C.full, C.at(f"G4{2 * n + d}"))
                    pool.tensor_tensor(heads(Z[d][10]), K_[:, tiles[d]], scaled(kds, d), ALU.mult)\
                        .then_inc(S("kd_scaled"), 1)
            experts(1)

        @block.scalar
        def _(act):
            def chain(ins):
                chained[0] += 1
                ins.then_inc(S("act_chain"), 1)
                act.wait_ge(S("act_chain"), chained[0])

            chained = [0]
            A = act.activation

            def take(name):
                act.wait_ge(C.full, C.at(name))
                return C.bank(name)

            def take_root(name, dst, width, n=T):
                b = take(name)
                A(dst, b[:, 0:n], ACT.Sqrt, bias=eps, scale=1.0 / width).then_inc(C.free, 1)

            act.wait_ge(S("params"), 16 * 2)
            act.wait_ge(S("consts"), 2)
            A(cs, par[:, PCOL["cvec"][0]:PCOL["cvec"][0] + 2 * KD], ACT.Silu).then_inc(S("silu_c"), 1)
            act.wait_ge(S("lam_neg"), 1)
            chain(A(lamt[:, 0:2], lamt[:, 0:2], ACT.Exp))
            A(lamt[:, 0:2], lamt[:, 0:2], ACT.Ln, bias=one).then_inc(S("lam_ln"), 1)
            A(nega, pcol("alog", 0, 8), ACT.Exp).then_inc(S("lam_ln"), 1)
            act.wait_ge(S("x_in"), 16)
            for k in range(KD):
                A(sq8[:, k, :], xT[:, k, :], ACT.Square).then_inc(S("sq_x"), 1)
            take_root("ss_x", root[:, 0, :], D)

            def qk_root(n):
                if n >= 4:
                    act.wait_ge(S("qk_ready"), n - 3)
                take_root(f"ss_qk{n}", root[:, n % 4, :], HD)

            for n in range(8):
                act.wait_ge(V.free, V.at(f"qk{n}"))
                if n >= 2:
                    act.wait_ge(C.full, C.at(f"ss_qk{n - 2}"))
                A(sq2[:, n % 2, :], qk[:, n, :], ACT.Square).then_inc(S("sq_qk"), 1)
                if n:
                    qk_root(n - 1)

            for s in range(TT):
                A(vtok[:, s, :], take(f"v{s}")[:, :], ACT.Copy).then_inc(C.free, 1)
                if s == 0:
                    qk_root(7)
            act.wait_ge(S("mod_out"), 16 * 4)
            for c in range(2):
                A(xge[:, c, :], take(f"xg{c}")[:, :], ACT.Gelu_apprx_tanh).then_inc(C.free, 1)
            for c in range(2):
                A(gsig[:, c, :], take(f"cg{c}")[:, :], ACT.Sigmoid).then_inc(C.free, 1)

            def softplus(h):
                z = zbanks[h % 2]
                act.wait_ge(S("z_ready"), h + 1)
                if h:
                    act.wait_ge(S("sp_raw"), 3 * h)
                else:
                    act.wait_ge(S("qk_ready"), 8)
                for b, w in ((0, 512), (1, 512), (2, 256)):
                    last = A(lnb[:, 512 * b:512 * b + w], z[b][:, 0:w], ACT.Abs)
                chain(last)
                chain(A(lnb, lnb, ACT.Exp, scale=-1.0))
                A(lnb, lnb, ACT.Ln, bias=one).then_inc(S("ln_ready"), 1)

            softplus(0)
            for h in range(NH):
                if h + 1 < NH:
                    softplus(h + 1)
                z = zbanks[h % 2]
                act.wait_ge(S("arg_ready"), h + 1)
                if h >= 2:
                    act.wait_ge(S("o_ready"), h - 1)
                for b, w in ((0, 512), (1, 512), (2, 256)):
                    A(wb[h % 2][:, 512 * b:512 * b + w], z[b][:, 0:w], ACT.Exp).then_inc(S("w_raw"), 1)

            act.wait_ge(S("w_ready"), NH)
            act.wait_ge(S("lam8"), 1)
            for c in range(2):
                A(lr[:, c, :], take(f"lru{c}0")[:, :], ACT.Sigmoid, bias=pcol("lba", c)).then_inc(C.free, 1)
                A(li[:, c, :], take(f"lru{c}1")[:, :], ACT.Sigmoid, bias=pcol("lbx", c)).then_inc(C.free, 1)
            act.wait_ge(C.free, C.at("lru11"))
            for c in range(2):
                A(lt_[:, c, :], lr[:, c, :], ACT.Tanh, scale=lam8[:, c:c + 1]).then_inc(S("lru_ta"), 1)
            act.wait_ge(S("ln_centred"), 2)
            for c in range(2):
                A(sq2[:, c, :], dwo[:, c, :], ACT.Square).then_inc(S("sq_ln"), 1)
            for c in range(2):
                A(la[:, c, :], lr[:, c, :], ACT.Exp, scale=lam8[:, c:c + 1]).then_inc(S("lru_ta"), 1)
            take_root("ss_ln", root[:, 2, :], 256)
            act.wait_ge(S("lru_q"), 1)
            A(lt_, lt_, ACT.Sqrt).then_inc(S("lru_s"), 1)
            act.wait_ge(S("ln_scaled"), 2)
            for c in range(2):
                A(lnx[:, c, :], lnx[:, c, :], ACT.Silu, bias=pcol("lnb", c), scale=pcol("lng", c)).then_inc(S("ln_silu"), 1)
            for e in range(2):
                A(dwo[:, e, :], take(f"pw{e}")[:, :], ACT.Identity, bias=pcol("pwb", e)).then_inc(C.free, 1)
            act.wait_ge(C.free, C.at("pw1"))
            act.wait_ge(S("o_taken"), 4)
            act.wait_ge(S("yb_ready"), 2)
            for k in range(KD):
                A(sq8[:, k, :], yT[:, k, :], ACT.Square).then_inc(S("sq_y"), 1)
            for i, (name, w) in enumerate((("ss_a", 512), ("ss_b", 256), ("ss_c", 256))):
                if i == 2:
                    act.wait_ge(S("ln_scaled"), 2)
                take_root(name, root[:, i, :], w)

            def norm_tok(ready, squares=xn_tok):
                for t in range(TT):
                    ready(t)
                    ins = A(squares[:, t, :], x_tok[:, t, :], ACT.Square, accum_out=ssq[:, t:t + 1])
                    chain(ins)
                A(rstd, ssq, ACT.Sqrt, bias=eps, scale=1.0 / D).then_inc(S("rms_ready"), 1)

            def turned(tag, dst, gain, shift):
                for k in range(KD):
                    b = take(f"{tag}{k}")
                    if shift is None:
                        A(dst[:, k, :], b[:, :], ACT.Copy, scale=gain[:, k:k + 1]).then_inc(C.free, 1)
                    else:
                        A(dst[:, k, :], b[:, :], ACT.Identity, scale=gain[:, k:k + 1],
                          bias=shift[:, k:k + 1]).then_inc(C.free, 1)

            def experts(m):
                act.wait_ge(S("coarse"), m + 1)
                A(ex, ex, ACT.Exp).then_inc(S("coarse_exp"), 1)
                act.wait_ge(S("fine"), m + 1)
                A(ev, dv, ACT.Exp).then_inc(S("fine_exp"), 1)

                def store(b, q):
                    for half in range(2):
                        src = ys[q][CAP * half:CAP * half + CAP, :]
                        if isinstance(b, int):
                            dst = yd[m][CAP * b:CAP * b + CAP, 512 * half:512 * half + 512]
                        else:
                            dst = yd[m].rearrange("(b s) d -> b s d", s=CAP)[bass.ds(b, 1), :, 512 * half:512 * half + 512]\
                                .rearrange("b s d -> (b s) d")
                        act.dma_start(dst, src).then_inc(stored(q), 16)

                def stored(q):
                    return S(f"stored{q}")

                def take_y(e, q, w):
                    n = NE * m + e
                    act.wait_ge(S("y_done"), n + 1)
                    positive(act, stored(q), w)
                    A(ys[q], Y[q][:, :], ACT.Copy).then_inc(S("y_taken"), 1)
                    act.wait_ge(S("y_taken"), n + 1)
                    store(e, q)

                def step(e, q, i=None):
                    n = NE * m + e
                    positive(act, S("gu_done"), n + 1)
                    positive(act, S("h_done"), n - 1)
                    A(sg[q][CAP:2 * CAP, :], GU[q][0:CAP, :], ACT.Silu).then_inc(S("silu_done"), 1)
                    if i is not None:
                        take_y(e - 1, 1 - q, 32 * (NE // 2 * m) + (i + q) * 32)
                    elif e:
                        take_y(e - 1, 1 - q, 32 * (NE // 2 * m + (e - 1) // 2))
                    positive(act, S("ht_done"), n + 1)
                    A(hTs[q], HT[q][:, 0:4 * CAP], ACT.Copy).then_inc(S("hts_ready"), 1)

                step(0, 0)
                step(1, 1)
                step(2, 0)
                step(3, 1)
                with nc.scalar.Fori(2, NE // 2) as i:
                    for q in range(2):
                        step(i * 2 + q, q, i - 1)
                take_y(NE - 1, 1, 32 * (NE // 2 * (m + 1) - 1))
                baton = S(f"beyond{m}")
                act.wait_ge(S("routed"), m + 1)
                act.wait_ge(S("stored0"), 32 * (NE // 2) * (m + 1))
                n_over = act.value_load(ovt[0:1, NOV:NOV + 1], min_val=0, max_val=NOV)
                act.sem_inc(S(f"beyond_st{m}"), 32)
                with nc.scalar.Fori(0, NOV) as i:
                    with act.If(n_over > i):
                        act.wait_ge(baton, i * 8 + 20)
                        A(sg[0][CAP:2 * CAP, :], GU[0][0:CAP, :], ACT.Silu).then_inc(baton, 1)
                        act.wait_ge(baton, i * 8 + 23)
                        A(hTs[0], HT[0][:, 0:4 * CAP], ACT.Copy).then_inc(baton, 1)
                        act.wait_ge(S(f"beyond_y{m}"), i + 3)
                        A(ys[0], Y[0][:, :], ACT.Copy).then_inc(baton, 1)
                        act.wait_ge(baton, i * 8 + 25)
                        for half in range(2):
                            dst = yd[m].rearrange("(b s) d -> b s d", s=CAP)[bass.ds(i + NE, 1), :, 512 * half:512 * half + 512]\
                                .rearrange("b s d -> (b s) d")
                            act.dma_start(dst, ys[0][CAP * half:CAP * half + CAP, :]).then_inc(S(f"beyond_st{m}"), 16)
                        settle(act, S(f"beyond_st{m}"), (i + 2) * 32)

            norm_tok(lambda t: act.wait_ge(V.free, V.at(f"outA1{t}")))
            act.wait_ge(S("gains"), 1)
            turned("turn0_", hT3, mAn, None)
            experts(0)

            act.wait_ge(S("ctx_in"), 16)
            for k in range(KD):
                A(csq[:, k, :], hTc[:, k, :], ACT.Square).then_inc(S("sq_ctx"), 1)
            take_root("ss_ctx", croot, D, n=CTX)
            norm_tok(lambda t: act.wait_ge(S("x2_ready"), t + 1), chunks(area(3, 0, 4096), D))
            act.wait_ge(S("xn2"), TT)
            turned("turnX", hT0, aX, mc[:, MC.index("x0"), :])
            for g in range(4):
                A(fT[:, g, :], take(f"f{g}")[:, :], ACT.Copy).then_inc(C.free, 1)
            act.wait_ge(S("x2_out"), 16)
            for s in range(TT):
                A(AB[:, s, 2:4, :], take(f"ab{s}1")[:, :].rearrange("p (g n) -> p g n", g=2), ACT.Copy).then_inc(C.free, 1)

            def roots2(n):
                if n >= 1:
                    act.wait_ge(S("norm2x"), n)
                take_root(f"ssx{n}", rootn, 1)
                if n >= 4:
                    if n > 4:
                        act.wait_ge(S("norm2c"), n - 4)
                    take_root(f"ssc{n}", rootc, 1, n=CTX)

            def turned2(n):
                h = n % 4
                kt, ktc = (Ktok, Kc) if n < 8 else (Vtok, Vc)
                A(kt[:, :, h, :], chunks(take(f"tx{n}")[:, :], P), ACT.Copy).then_inc(C.free, 1)
                A(ktc[:, :, h, :], chunks(take(f"tc{n}")[:, 0:CTX], P), ACT.Copy).then_inc(C.free, 1)

            act.wait_ge(S("gates_in"), 1)
            A(beta, gt[:, :, 0:8], ACT.Sigmoid).then_inc(S("beta"), 1)
            act.wait_ge(S("gate_neg"), 1)
            chain(A(gtot, gtot, ACT.Exp))
            A(gtot, gtot, ACT.Ln, bias=one).then_inc(S("gate_ln"), 1)
            for n in range(14):
                if n == 2:
                    act.wait_ge(S("cums_in"), 1)
                    A(egl, gtot, ACT.Exp).then_inc(S("gate_exp"), 1)
                    A(kbs, gcum, ACT.Exp).then_inc(S("gate_exp"), 1)
                    A(kds, kds, ACT.Exp).then_inc(S("gate_exp"), 1)
                if n < 12:
                    act.wait_ge(S("conv2x"), n + 1)
                    ins = A(co[n % 2], co[n % 2], ACT.Silu)
                    if n < 8:
                        chain(ins)
                        if n:
                            act.wait_ge(C.full, C.at(f"ssx{n - 1}"))
                        A(sqn, co[n % 2], ACT.Square).then_inc(S("sq2x"), 1)
                    else:
                        ins.then_inc(S("vx"), 1)
                    if n >= 4:
                        act.wait_ge(S("conv2c"), n - 3)
                        ins = A(coc[n % 2], coc[n % 2], ACT.Silu)
                        if n < 8:
                            chain(ins)
                            if n > 4:
                                act.wait_ge(C.full, C.at(f"ssc{n - 1}"))
                            A(sqc, coc[n % 2], ACT.Square).then_inc(S("sq2c"), 1)
                        else:
                            ins.then_inc(S("vc"), 1)
                if n in (4, 6, 8, 10):
                    c = n // 2 - 2
                    A(zT[:, c, :], take(f"z{c}")[:, :], ACT.Silu).then_inc(C.free, 1)
                if 1 <= n <= 8:
                    roots2(n - 1)
                if n >= 6:
                    turned2(n - 2)
            for n, (isc, _) in enumerate(pairs):
                both = [(2 * n + d, Z[d]) for d in range(2)]

                def copy(name, si, dst):
                    A(dst, take(f"{name}{si}")[:, :], ACT.Copy).then_inc(C.free, 1)

                for si, z in both:
                    copy("row", si, z[1])
                    if not isc:
                        act.wait_ge(C.free, C.at(f"row{si}"))
                        A(z[2], z[1], ACT.Exp).then_inc(S("rows_exp"), 1)
                for si, z in both:
                    act.wait_ge(S("dec_arg"), si + 1)
                    A(z[0], z[0], ACT.Exp, scale=-1.0).then_inc(S("dec_exp"), 1)
                    if not isc:
                        A(z[3], z[3], ACT.Exp).then_inc(S("dect_exp"), 1)
                for stage_ in ((("D2", 4), ("D2T", 9)), (("D4", 10), ("D4T", 11)), (("D8", 11),), (("G", 0),),
                               (("RV", 7), ("RK", 8)), (("G2", 10), ("G2T", 11)), (("G4", 11),),
                               (("U", 0), ("WT", 4))):
                    for si, z in both:
                        for name, i in stage_:
                            copy(name, si, z[i])
            act.wait_ge(S("o_done"), 2 * TT)
            for h in range(4):
                A(Z[0][h], y2T[:, 4 + h, :], ACT.Square).then_inc(S("sq_o"), 1)
            for h in range(4):
                take_root(f"so{h}", Z[0][4 + h], P)

            norm_tok(lambda t: act.wait_ge(V.free, V.at(f"outB1{TT - 1}")))
            turned("turn1_", hT3, mAn, mBn)
            experts(1)
            for t in range(TT):
                act.wait_ge(S("x4_ready"), t + 1)
                if t >= 2:
                    act.wait_ge(S(f"out{t % 2}"), 16 * (t // 2))
                chain(A(fin[t % 2], x_tok[:, t, :], ACT.Square, accum_out=ssq[:, t:t + 1]))
                A(rstd[:, t:t + 1], ssq[:, t:t + 1], ACT.Sqrt, bias=eps, scale=1.0 / D).then_inc(S("rms4"), 1)

        @block.vector
        def _(dve):
            chained = [0]

            def chain(ins):
                chained[0] += 1
                ins.then_inc(S("dve_chain"), 1)
                dve.wait_ge(S("dve_chain"), chained[0])

            def take(name):
                dve.wait_ge(V.full, V.at(name))
                return V.bank(name)

            def own(name):
                dve.wait_ge(V.free, V.at(name))

            def thin(name, n, sizes, buf):
                at = 0
                for i, size in enumerate(sizes):
                    b = take(f"{name}T{i}")
                    o = buf[0:n, at:at + size]
                    chain(CP(o, b[64:64 + n, 0:size]))
                    TTo(o, b[0:n, 0:size], o, ALU.add).then_inc(V.free, 1)
                    at += size

            TTo, TS, STT, CP = dve.tensor_tensor, dve.tensor_scalar, dve.scalar_tensor_tensor, dve.tensor_copy
            dve.memset(zeros, 0.0).then_inc(S("zeros"), 1)
            dve.memset(eps, EPS).then_inc(S("consts"), 1)
            dve.memset(one, 1.0).then_inc(S("consts"), 1)
            dve.memset(upad[:, :, 0:FW - 1], 0.0)
            chain(dve.memset(xrp[:, :, 0:CW - 1], 0.0))
            dve.wait_ge(S("params"), 16 * 2)
            STT(lamt[:, 0:2], pcol("lam", 0, 2), -1.0, pcol("lam", 0, 2), ALU.mult, ALU.min).then_inc(S("lam_neg"), 1)
            TS(lamt[:, 2:4], pcol("lam", 0, 2), 0.0, 8.0, ALU.min, ALU.mult)
            chain(TS(gq8, pcol("gq"), HD ** -0.5, None, ALU.mult))
            dve.wait_ge(S("lam_ln"), 2)
            STT(lam8, lamt[:, 0:2], -8.0, lamt[:, 2:4], ALU.mult, ALU.add).then_inc(S("lam8"), 1)
            chain(TS(nega, nega, -1.0, None, ALU.mult))

            def modulation(n0, n1):
                for n in range(n0, n1):
                    b = take(f"mod{n}")
                    for g in range(4):
                        ins = CP(modv[32 * g:32 * g + 2, P * n:P * n + P], b[32 * g:32 * g + 2, 0:P])
                    ins.then_inc(V.free, 1)

            modulation(0, 1)
            dve.wait_ge(C.free, C.at("ss_x"))
            chain(dve.reciprocal(root[:, 0, :], root[:, 0, :]))
            for k in range(KD):
                STT(xT[:, k, :], xT[:, k, :], pcol("g1", k), root[:, 0, :], ALU.mult, ALU.mult)\
                    .then_inc(S("h_ready"), 1)
            dve.wait_ge(S("h_ready"), KD)

            def qk_norm(n):
                dve.wait_ge(C.free, C.at(f"ss_qk{n}"))
                chain(dve.reciprocal(root[:, n % 4, :], root[:, n % 4, :]))
                STT(qk[:, n, :], qk[:, n, :], gq8 if n < 4 else pcol("gk"), root[:, n % 4, :], ALU.mult, ALU.mult)\
                    .then_inc(S("qk_ready"), 1)

            for n in range(8):
                if n == 4:
                    modulation(1, 4)
                CP(qk[:, n, :], take(f"qk{n}")[:, :]).then_inc(V.free, 1)
                if n:
                    qk_norm(n - 1)
            modulation(4, 8)
            qk_norm(7)
            modulation(8, 12)
            for c in range(2):
                CP(xrp[:, c, CW - 1:], take(f"xr{c}")[:, :]).then_inc(V.free, 1)
            for c in range(2):
                b = take(f"cv{c}")
                dve.wait_ge(C.free, C.at(f"cg{c}"))
                TTo(upad[:, c, FW - 1:], b[:, :], gsig[:, c, :], ALU.mult).then_inc(V.free, 1)
            own("cv1")

            def lru_conv():
                for c in range(2):
                    o = xconv[:, c, :]
                    chain(TS(o, xrp[:, c, 0:T], pcol("lcw", CW * c), pcol("lcb", c), ALU.mult, ALU.add))
                    for j in range(1, CW):
                        ins = STT(o, xrp[:, c, j:j + T], pcol("lcw", CW * c + j), o, ALU.mult, ALU.add)
                        if j < CW - 1:
                            chain(ins)
                    ins.then_inc(S("xconv"), 1)

            def conv_tap(k):
                c, j = k // FW, k % FW
                o = dwo[:, c, :]
                if j == 0:
                    chain(TS(o, upad[:, c, 0:T], pcol("dww", FW * c), pcol("dwb", c), ALU.mult, ALU.add))
                else:
                    ins = STT(o, upad[:, c, j:j + T], pcol("dww", FW * c + j), o, ALU.mult, ALU.add)
                    if j < FW - 1:
                        chain(ins)
                    else:
                        ins.then_inc(S("dwconv"), 1)

            for h in range(NH):
                z = zbanks[h % 2]
                dve.wait_ge(S("ln_ready"), h + 1)
                if h >= 2:
                    dve.wait_ge(S("arg_ready"), h - 1)
                for b, w in ((0, 512), (1, 512), (2, 256)):
                    s_ = slice(512 * b, 512 * b + w)
                    STT(spb[h % 2][:, s_], z[b][:, 0:w], 0.0, lnb[:, s_], ALU.max, ALU.add).then_inc(S("sp_raw"), 1)
                if h >= 2 and h % 2 == 0:
                    dve.wait_ge(S("o_ready"), h)
                    CP(yT[:, h // 2 - 1, :], psum[6 + (h // 2 - 1) % 2][:, :]).then_inc(S("o_taken"), 1)
                if h == 0:
                    lru_conv()
                for k in range(8 * h, min(8 * h + 8, 2 * FW)):
                    conv_tap(k)
            dve.wait_ge(S("o_ready"), NH)
            CP(yT[:, 3, :], psum[7][:, :]).then_inc(S("o_taken"), 1)
            b = take("mu")
            dve.wait_ge(S("dwconv"), 2)
            for c in range(2):
                ins = STT(dwo[:, c, :], b[:, :], -1.0 / 256, dwo[:, c, :], ALU.mult, ALU.add).then_inc(S("ln_centred"), 1)
            dve.wait_ge(S("ln_centred"), 2)
            dve.sem_inc(V.free, 1)
            dve.wait_ge(S("lru_ta"), 2)
            chain(TS(ld, lt_, -1.0, 1.0, ALU.mult, ALU.add))
            chain(dve.reciprocal(ld, ld))
            STT(lt_, lt_, -2.0, ld, ALU.mult, ALU.mult).then_inc(S("lru_q"), 1)
            chain(TTo(li, li, xconv, ALU.mult))
            dve.wait_ge(C.free, C.at("ss_ln"))
            chain(dve.reciprocal(root[:, 2, :], root[:, 2, :]))
            dve.wait_ge(S("yd_zero"), 16 * 2)
            for c in range(2):
                TTo(lnx[:, c, :], dwo[:, c, :], root[:, 2, :], ALU.mult).then_inc(S("ln_scaled"), 1)
            dve.wait_ge(S("lru_s"), 1)
            dve.wait_ge(S("lru_ta"), 4)
            chain(TTo(li, li, lt_, ALU.mult))
            for c in range(2):
                ins = dve.tensor_tensor_scan(out=lr[:, c, :], data0=la[:, c, :], data1=li[:, c, :], initial=0.0,
                                             op0=ALU.mult, op1=ALU.add)
            chain(ins)
            for c in range(2):
                TTo(xconv[:, c, :], lr[:, c, :], xge[:, c, :], ALU.mult).then_inc(S("yb_ready"), 1)
            for i, (name, k0, k1) in enumerate((("ss_a", 0, 4), ("ss_b", 4, 6), ("ss_c", 6, 8))):
                dve.wait_ge(C.free, C.at(name))
                chain(dve.reciprocal(root[:, i, :], root[:, i, :]))
                for k in range(k0, k1):
                    STT(yT[:, k, :], yT[:, k, :], pcol("gout", k), root[:, i, :], ALU.mult, ALU.mult)\
                        .then_inc(S("outA_ready"), 1)
            dve.wait_ge(S("x_again"), 16)
            for n in range(2):
                for t in range(TT):
                    o = x_tok[:, t, 512 * n:512 * n + 512]
                    TTo(o, take(f"outA{n}{t}")[:, :], o, ALU.add).then_inc(V.free, 1)

            def norm_tok(i, m):
                dve.wait_ge(S("rms_ready"), i)
                chain(dve.reciprocal(rstd, rstd))
                for t in range(TT):
                    TS(xn_tok[:, t, :], x_tok[:, t, :], rstd[:, t:t + 1], None, ALU.mult).then_inc(S(f"xn{m}"), 1)

            def experts(m):
                gain, shift = mAp, (mBp if m else None)
                thin(f"logits{m}", NR, [T], logitsT)
                b = take(f"logits{m}")
                L3 = b[:, 0:TT * NR].rearrange("p (t n) -> p t n", n=NR)
                if m:
                    TTo(lg, L3, bc(pcol("rbias", 0, NR), 1, [P, TT, NR]), ALU.add).then_inc(V.free, 1)
                else:
                    CP(lg, L3).then_inc(V.free, 1)
                own(f"logits{m}")
                lc = lg[:, :, 0:NG]
                chain(dve.tensor_reduce(cm, lc, AX, ALU.max))
                TTo(ex, lc, bc(cm, 2, [P, TT, NG]), ALU.subtract).then_inc(S("coarse"), 1)
                chain(TTo(oh, lc, bc(cm, 2, [P, TT, NG]), ALU.is_equal))
                chain(STT(t16, oh, -100.0, bc(pcol("io4", 0, NG), 1, [P, TT, NG]), ALU.mult, ALU.add))
                chain(dve.tensor_reduce(mn, t16, AX, ALU.min))
                TS(gi, mn, 100.0, None, ALU.add)
                chain(TTo(oh, t16, bc(mn, 2, [P, TT, NG]), ALU.is_equal))
                dve.wait_ge(S("coarse_exp"), m + 1)
                chain(dve.tensor_reduce(wg, ex, AX, ALU.add))
                dve.reciprocal(wg, wg)
                for t in range(TT):
                    ins = TTo(fm[:, t], lg[:, t, NG:NR].rearrange("p (g e) -> p g e", g=NG),
                              bc(oh[:, t, :], 2, [P, NG, EG]), ALU.mult)
                chain(ins)
                for t in range(TT):
                    ins = dve.tensor_reduce(fs[:, t, :], fm[:, t].rearrange("p g e -> p e g"), AX, ALU.add)
                chain(ins)
                for t in range(TT):
                    ins = dve.max(out=v8[:, t, :], in_=fs[:, t, :])
                chain(ins)
                TTo(dv, v8[:, :, 1], v8[:, :, 0], ALU.subtract).then_inc(S("fine"), 1)
                for t in range(TT):
                    ins = dve.max_index(out=idx8[:, t, :], in_max=v8[:, t, :], in_values=fs[:, t, :])
                chain(ins)
                chain(CP(eidf, idx8[:, :, 0:2]))
                chain(STT(eid, bc(gi, 2, [P, TT, 2]), float(EG), eidf, ALU.mult, ALU.add))
                io = bc(pcol("io32", 0, NE), 1, [P, TT, NE])
                TTo(m1, io, bc(eid[:, :, 0], 2, [P, TT, NE]), ALU.is_equal)
                chain(TTo(m2, io, bc(eid[:, :, 1], 2, [P, TT, NE]), ALU.is_equal))
                TTo(pick, m1, m2, ALU.add).then_inc(S("picked"), 1)
                dve.wait_ge(S("fine_exp"), m + 1)
                chain(TS(den, ev, 1.0, None, ALU.add))
                chain(dve.reciprocal(den, den))
                chain(TTo(w12[:, 0:TT], wg, den, ALU.mult))
                TTo(w12[:, TT:2 * TT], w12[:, 0:TT], ev, ALU.mult)
                b = take(f"rank{m}")
                CP(rk, b[:, 0:TT * NE].rearrange("p (t n) -> p t n", n=NE))
                CP(cnt, b[:, TT * NE:TT * NE + NE]).then_inc(V.free, 1)
                own(f"rank{m}")
                chain(TS(nov, cnt, float(CAP), None, ALU.is_gt))
                for j in range(2, T // CAP):
                    chain(STT(nov, cnt, float(CAP * j), nov, ALU.is_gt, ALU.add))
                chain(dve.tensor_tensor_scan(out=ove, data0=M["ones"][:, 0:NE], data1=nov, initial=0.0,
                                             op0=ALU.mult, op1=ALU.add))
                chain(TTo(b1, ove, nov, ALU.subtract))
                chain(STT(b1, b1, float(CAP), pcol("base1", 0, NE), ALU.mult, ALU.add))
                chain(STT(sm, rk, float(CAP), bc(b1, 1, [P, TT, NE]), ALU.is_ge, ALU.mult))
                chain(TTo(sm, sm, rk, ALU.add))
                chain(TTo(sm, sm, bc(pcol("base0", 0, NE), 1, [P, TT, NE]), ALU.add))
                TTo(m1, m1, sm, ALU.mult)
                chain(TTo(m2, m2, sm, ALU.mult))
                dve.tensor_reduce(s12[:, 0:TT], m1, AX, ALU.add)
                chain(dve.tensor_reduce(s12[:, TT:2 * TT], m2, AX, ALU.add))
                CP(sl, s12)
                at3 = [P, 2 * TT, NBLK + 1]
                chain(TTo(at_block, bc(s12, 2, at3), bc(pcol("slot0", 0, NBLK + 1), 1, at3), ALU.is_ge))
                dve.tensor_reduce(place, at_block, AX, ALU.add)
                chain(TTo(in_block, at_block[:, :, 0:NBLK], at_block[:, :, 1:NBLK + 1], ALU.subtract))
                for k in range(2):
                    o = in_block[:, TT * k:TT * k + TT, :]
                    TTo(o, o, bc(pcol("tokf", 0, TT), 2, [P, TT, NBLK]), ALU.mult)
                chain(STT(place, place, -float(CAP), s12, ALU.mult, ALU.add))
                TTo(in_place, bc(pcol("io64", 0, CAP), 1, [P, 2 * TT, CAP]), bc(place, 2, [P, 2 * TT, CAP]), ALU.is_equal)\
                    .then_inc(S("placed"), 1)
                chain(TTo(ovc, bc(ove[0:1], 1, [1, NOV, NE]), bc(pcol("io15", 0, NOV)[0:1], 2, [1, NOV, NE]), ALU.is_le))
                chain(dve.tensor_reduce(ovf[0:1, 0:NOV], ovc, AX, ALU.add))
                CP(ovf[0:1, NOV:NOV + 1], ove[0:1, NE - 1:NE])
                chain(TS(ovf[0:1, 0:NOV], ovf[0:1, 0:NOV], float(NE - 1), None, ALU.min))
                CP(ovt, ovf[0:1, 0:NOV + 1]).then_inc(S("routed"), 1)
                dve.sem_inc(S(f"beyond{m}"), 17)

                def affine_x(e, q):
                    n = NE * m + e
                    positive(dve, S("xt_done"), n + 1)
                    positive(dve, S("gu_done"), n - 1)
                    o = chunks(xTs[q], CAP)
                    ins = TTo(o, chunks(XT[q][:, :], CAP), bc(gain, 2, [P, KD, CAP]), ALU.mult)
                    if shift is not None:
                        ins.then_inc(S("x_gained"), 1)
                        positive(dve, S("x_gained"), e + 1)
                        ins = TTo(o, o, bc(shift, 2, [P, KD, CAP]), ALU.add)
                    ins.then_inc(S("xs_ready"), 1)

                def step(e, q, last=False):
                    n = NE * m + e
                    positive(dve, S("silu_done"), n + 1)
                    positive(dve, S("ht_done"), n - 1)
                    TTo(hb[q], sg[q][CAP:2 * CAP, :], GU[q][CAP:2 * CAP, :], ALU.mult).then_inc(S("h_done"), 1)
                    if not last:
                        affine_x(e + 1, 1 - q)

                CP(slots_tok, take(f"slots{m}")[0:CAP, 0:NBLK]).then_inc(V.free, 1)
                dve.wait_ge(S("gains"), 1 + 2 * m)
                affine_x(0, 0)
                step(0, 0)
                step(1, 1)
                with nc.vector.Fori(1, NE // 2 - 1) as i:
                    for q in range(2):
                        step(i * 2 + q, q)
                step(NE - 2, 0)
                step(NE - 1, 1, last=True)
                baton = S(f"beyond{m}")
                dve.wait_ge(S("routed"), m + 1)
                n_over = dve.value_load(ovt[0:1, NOV:NOV + 1], min_val=0, max_val=NOV)
                with nc.vector.Fori(0, NOV) as i:
                    with dve.If(n_over > i):
                        dve.wait_ge(baton, i * 8 + 18)
                        o = chunks(xTs[0], CAP)
                        ins = TTo(o, chunks(XT[0][:, :], CAP), bc(gain, 2, [P, KD, CAP]), ALU.mult)
                        if shift is not None:
                            ins.then_inc(S(f"beyond_g{m}"), 1)
                            dve.wait_ge(S(f"beyond_g{m}"), i + 1)
                            ins = TTo(o, o, bc(shift, 2, [P, KD, CAP]), ALU.add)
                        ins.then_inc(baton, 1)
                        dve.wait_ge(baton, i * 8 + 21)
                        TTo(hb[0], sg[0][CAP:2 * CAP, :], GU[0][CAP:2 * CAP, :], ALU.mult).then_inc(baton, 1)
                        settle(dve, baton, i * 8 + 25)

            norm_tok(1, 0)
            CP(mAp, pcol("g2p", 0, KD))
            CP(mAn, pcol("g2n", 0, KD)).then_inc(S("gains"), 1)
            experts(0)
            dve.wait_ge(S("mod_cols"), 16 * 8)
            chain(TTo(mc, mc, chunks(pcol("bmc", 0, 8 * KD), KD), ALU.add))
            for g, name, o in (("h1n", "x1", aX), ("h1n", "c1", aC), ("h2n", "x4", mAn), ("h2p", "x4p", mAp)):
                STT(o, mc[:, MC.index(name), :], 1.0, pcol(g, 0, KD), ALU.add, ALU.mult)
            CP(mBn, mc[:, MC.index("x3"), :])
            CP(mBp, mc[:, MC.index("x3p"), :]).then_inc(S("gains"), 1)
            dve.wait_ge(S("gains"), 2)
            for t in range(TT):
                dve.wait_ge(S(f"y_in{t % 2}"), 32 * (t // 2 + 1))
                o = x_tok[:, t, :]
                chain(STT(o, yg[t % 2][0], w12[:, t:t + 1], o, ALU.mult, ALU.add))
                ins = STT(o, yg[t % 2][1], w12[:, TT + t:TT + t + 1], o, ALU.mult, ALU.add)
                chain(ins)
                dve.sem_inc(S("combined0"), 1)
                dve.sem_inc(S("x2_ready"), 1)

            norm_tok(2, 2)
            dve.wait_ge(C.free, C.at("ss_ctx"))
            chain(dve.reciprocal(croot, croot))
            for k in range(KD):
                ins = TTo(hTc[:, k, :], hTc[:, k, :], croot, ALU.mult)
            chain(ins)
            for k in range(KD):
                TS(hTc[:, k, :], hTc[:, k, :], aC[:, k:k + 1], mc[:, MC.index("c0"), k:k + 1], ALU.mult, ALU.add)\
                    .then_inc(S("ctx_ready"), 1)
            dve.wait_ge(S("x2_out"), 16)
            for s in range(TT):
                CP(AB[:, s, 0:2, :], take(f"ab{s}0")[:, :].rearrange("p (g n) -> p g n", g=2)).then_inc(V.free, 1)
            for g in range(4):
                CP(y2T[:, g, :], take(f"dft{g}")[:, :]).then_inc(V.free, 1)
            for i in range(2):
                dve.memset(pad2[i], 0.0)
                ins = dve.memset(padc[i], 0.0)
            chain(ins)

            def norm2(n):
                dve.wait_ge(C.free, C.at(f"ssx{n}"))
                chain(dve.reciprocal(rootn, rootn))
                o = q2[:, n, :] if n < 4 else k2[:, n - 4, :]
                STT(o, co[n % 2], P ** -0.5 if n < 4 else 1.0, rootn, ALU.mult, ALU.mult).then_inc(S("norm2x"), 1)
                if n >= 4:
                    dve.wait_ge(C.free, C.at(f"ssc{n}"))
                    chain(dve.reciprocal(rootc, rootc))
                    TTo(kc[:, n - 4, :], coc[n % 2], rootc, ALU.mult).then_inc(S("norm2c"), 1)

            thin("gates", 16, [CTX, T], gatesT)
            CP(gt, take("gates")[:, 0:96].rearrange("p (t n) -> p t n", n=16)).then_inc(V.free, 1)
            own("gates")
            dve.sem_inc(S("gates_in"), 1)
            chain(TTo(gcum, gt[:, :, 8:16], bc(pcol("dtb", 0, 8), 1, [P, 6, 8]), ALU.add))
            STT(gtot, gcum, -1.0, gcum, ALU.mult, ALU.min).then_inc(S("gate_neg"), 1)
            dve.wait_ge(S("gate_ln"), 1)
            chain(STT(gval, gcum, 0.0, gtot, ALU.max, ALU.add))
            TTo(gval, gval, bc(nega, 1, [P, 6, 8]), ALU.mult).then_inc(S("gval"), 1)
            for n in range(12):
                if n == 1:
                    b = take("cums")
                    CP(gcum, b[:, 0:48].rearrange("p (t n) -> p t n", n=8))
                    CP(gtot, b[:, 48:96].rearrange("p (t n) -> p t n", n=8)).then_inc(V.free, 1)
                    own("cums")
                    TTo(kds, gtot, gcum, ALU.subtract).then_inc(S("cums_in"), 1)
                if n == 3:
                    dve.wait_ge(S("gate_exp"), 3)
                    dve.wait_ge(S("beta"), 1)
                    TTo(kbs, kbs, beta, ALU.mult).then_inc(S("cols2"), 1)
                pad, o = pad2[n % 2], co[n % 2]
                o8 = o.rearrange("p (r c) -> p r c", c=64)
                CP(pad[:, 1:9, 1:65], take(f"px{n}")[:, :].rearrange("p (r c) -> p r c", c=64)).then_inc(V.free, 1)
                if n >= 4:
                    CP(padc[n % 2][:, 1:CTX + 1], take(f"pc{n}")[:, 0:CTX]).then_inc(V.free, 1)
                    own(f"pc{n}")
                else:
                    own(f"px{n}")
                if n >= 10:
                    dve.wait_ge(C.full, C.at(f"tc{n - 2}"))
                elif n >= 2:
                    dve.wait_ge(S("norm2x"), n - 1)
                chain(TS(o8, pad[:, 0:8, 0:64], pcol("cw2", 9 * n), None, ALU.mult))
                for j in range(1, 9):
                    ins = STT(o8, pad[:, j // 3:j // 3 + 8, j % 3:j % 3 + 64], pcol("cw2", 9 * n + j), o8,
                              ALU.mult, ALU.add)
                    if j < 8:
                        chain(ins)
                ins.then_inc(S("conv2x"), 1)
                if n >= 4:
                    oc, pc = coc[n % 2], padc[n % 2]
                    chain(TS(oc, pc[:, 0:CTX], pcol("cw2", 9 * n + 3), None, ALU.mult))
                    chain(STT(oc, pc[:, 1:CTX + 1], pcol("cw2", 9 * n + 4), oc, ALU.mult, ALU.add))
                    STT(oc, pc[:, 2:CTX + 2], pcol("cw2", 9 * n + 5), oc, ALU.mult, ALU.add).then_inc(S("conv2c"), 1)
                if 1 <= n <= 8:
                    norm2(n - 1)
            dve.wait_ge(C.full, C.at("tc11"))
            for d in range(2):
                ins = dve.memset(St[d], 0.0)
            chain(ins)

            for n, (isc, tiles) in enumerate(pairs):
                both = [(d, 2 * n + d, Z[d], tiles[d] if isc else TC + tiles[d]) for d in range(2)]

                def cols4(col, d, tau):
                    return bc(col[:, tau, 4 * d:4 * d + 4], 2, [P, 4, P])

                def mat4(name):
                    return bc(M[name], 1, [P, 4, P])

                def plus(name, i):
                    for d, si, z, tau in both:
                        TTo(z[i], take(f"{name}{si}")[:, :], z[i], ALU.add).then_inc(V.free, 1)

                for d, si, z, tau in both:
                    dve.wait_ge(C.free, C.at(f"row{si}"))
                    chain(TTo(heads(z[0]), heads(z[1]), cols4(gcum, d, tau), ALU.subtract))
                    if not isc:
                        TS(z[3], z[0], 0.0, None, ALU.min)
                    TS(z[0], z[0], 0.0, None, ALU.max).then_inc(S("dec_arg"), 1)
                for d, si, z, tau in both:
                    dve.wait_ge(S("dec_exp"), si + 1)
                    TTo(z[4], take(f"kk{si}")[:, :], z[0], ALU.mult).then_inc(V.free, 1)
                    own(f"kk{si}")
                    chain(TTo(heads(z[4]), heads(z[4]), cols4(beta, d, tau), ALU.mult))
                    TTo(heads(z[5]), heads(z[4]), mat4("gtd" if d == 0 else "ltd"), ALU.mult)
                    TTo(heads(z[6]), heads(z[4]), mat4("gtl" if d == 0 else "ltl"), ALU.mult)\
                        .then_inc(S("dl_ready"), 1)
                if not isc:
                    for d, si, z, tau in both:
                        dve.wait_ge(S("dect_exp"), si - 2 * TC + 1)
                        TTo(z[3], take(f"kq{si}")[:, :], z[3], ALU.mult).then_inc(V.free, 1)
                        own(f"kq{si}")
                        chain(TTo(heads(z[3]), heads(z[3]), mat4("le" if d == 0 else "ge"), ALU.mult))
                for d, si, z, tau in both:
                    b = take(f"DT{si}")
                    CP(z[0], b[:, :])
                    TTo(heads(z[1]), mat4("ident"), heads(b[:, :]), ALU.subtract).then_inc(V.free, 1)
                own(f"DT{2 * n + 1}")
                for name in ("F1", "F2", "F3"):
                    plus(name, 1)
                for d, si, z, tau in both:
                    b = take(f"GT{si}")
                    CP(z[4], b[:, :])
                    TTo(heads(z[9]), mat4("ident"), heads(b[:, :]), ALU.subtract).then_inc(V.free, 1)
                own(f"GT{2 * n + 1}")
                plus("H1", 9)
                plus("H2", 9)
                for d, si, z, tau in both:
                    b = take(f"WS{si}")
                    dve.wait_ge(C.free, C.at(f"U{si}"))
                    TTo(z[6], z[0], b[:, :], ALU.subtract).then_inc(V.free, 1)
                own(f"WS{2 * n + 1}")
                if not isc:
                    for d, si, z, tau in both:
                        o = y2T[:, 4:8, P * tiles[d]:P * tiles[d] + P]
                        b = heads(take(f"OT{si}")[:, :])
                        ins = CP(o, b) if si - 2 * TC < TT else TTo(o, b, o, ALU.add)
                        ins.then_inc(V.free, 1)
                    own(f"OT{2 * n + 1}")
                    dve.sem_inc(S("o_done"), 2)
                for d, si, z, tau in both:
                    b = take(f"SU{si}")
                    chain(TTo(heads(St[d]), heads(St[d]), cols4(egl, d, tau), ALU.mult))
                    TTo(St[d], b[:, :], St[d], ALU.add).then_inc(V.free, 1)
            own(f"SU{LAST}")
            for h in range(4):
                o = y2T[:, 4 + h, :]
                dve.wait_ge(C.free, C.at(f"so{h}"))
                chain(dve.reciprocal(Z[0][4 + h], Z[0][4 + h]))
                chain(STT(o, o, pcol("onorm"), Z[0][4 + h], ALU.mult, ALU.mult))
                TTo(o, o, zT[:, h, :], ALU.mult).then_inc(S("outB_ready"), 1)
            dve.wait_ge(S("x2_again"), 48)
            chain(TTo(g2row, g2row, b2row, ALU.add))
            for n in range(2):
                for t in range(TT):
                    i = TT * n + t
                    o = x_tok[:, t, 512 * n:512 * n + 512]
                    chain(TTo(mixt[i % 2], take(f"outB{n}{t}")[:, :], g2row[:, 512 * n:512 * n + 512], ALU.mult))
                    TTo(o, mixt[i % 2], o, ALU.add).then_inc(V.free, 1)
            own(f"outB1{TT - 1}")
            norm_tok(3, 1)
            dve.sem_inc(S("gains"), 1)
            experts(1)
            dve.wait_ge(S("rows"), 48)
            chain(TTo(m5row, m5row, b5row, ALU.add))
            for t in range(TT + 1):
                if t < TT:
                    dve.wait_ge(S(f"y_in{t % 2}"), 32 * (2 + t // 2 + 1))
                    y0, y1 = yg[t % 2]
                    o = x_tok[:, t, :]
                    chain(TS(y0, y0, w12[:, t:t + 1], None, ALU.mult))
                    chain(STT(y0, y1, w12[:, TT + t:TT + t + 1], y0, ALU.mult, ALU.add))
                    chain(TTo(y0, y0, m5row, ALU.mult))
                    chain(TTo(o, o, y0, ALU.add))
                    dve.sem_inc(S("combined1"), 1)
                    dve.sem_inc(S("x4_ready"), 1)
                if t:
                    s = t - 1
                    dve.wait_ge(S("rms4"), t)
                    chain(dve.reciprocal(rstd[:, s:s + 1], rstd[:, s:s + 1]))
                    STT(fin[s % 2], x_tok[:, s, :], rstd[:, s:s + 1], fgrow, ALU.mult, ALU.mult)\
                        .then_inc(S("out_ready"), 1)


def square_matrices():
    import numpy as np

    p, f = np.arange(P)[:, None], np.arange(P)[None, :]
    same = p // 16 == f // 16
    m = {
        "ident": p == f, "ones": p == p + 0 * f, "lt": p < f, "le": p <= f, "ge": p >= f,
        "gtd": (p > f) & same, "ltd": (p < f) & same, "gtl": (p > f) & ~same, "ltl": (p < f) & ~same,
        "blk": p // HD == f // HD, "nge": -1.0 * (p >= f), "nones": -1.0 + 0 * (p + f),
    }
    return np.concatenate([np.broadcast_to(m[n], (P, P)).astype(np.float32) for n in MATS], axis=1)


def fourier_tables():
    import numpy as np

    c = np.arange(P)
    wc = 2 * np.pi * np.outer(c, c) / P
    t = np.arange(T)
    wt = 2 * np.pi * (np.outer(t, t) % T) / T
    chan = np.concatenate([np.cos(wc), np.sin(wc)], axis=1) / (P * T) ** 0.5
    pos = np.concatenate([np.cos(wt), -np.sin(wt)], axis=0)
    return chan.astype(np.float32), pos.astype(np.float32)


def kernel(**inputs):
    import numpy as np
    import concourse.bacc as bacc
    from concourse.bass_utils import run_bass_kernel_spmd

    i = {k: np.asarray(v) for k, v in inputs.items()}
    f32 = np.float32

    def nat(v):
        return v.reshape(-1, P).T

    def perm(v):
        return v.reshape(P, -1)

    def rows(v):
        return np.broadcast_to(v.reshape(1, -1), (P, v.size))

    def taps(w):
        return w.reshape(w.shape[0], -1, P).transpose(2, 1, 0).reshape(P, -1)

    parts = {
        "g1": nat(i["norm1_g"][0]), "gq": np.tile(i["q_norm_g"][0], 2)[:, None],
        "gk": np.tile(i["k_norm_g"][0], 2)[:, None], "lcw": taps(i["lru_conv_w"][0]),
        "lcb": nat(i["lru_conv_b"][0]), "lba": nat(i["lru_ba"][0]), "lbx": nat(i["lru_bx"][0]),
        "lam": nat(i["lru_lambda"][0]), "dww": taps(i["conf_dw_w"][0]), "dwb": nat(i["conf_dw_b"][0]),
        "lng": nat(i["conf_ln_g"][0]), "lnb": nat(i["conf_ln_b"][0]), "pwb": nat(i["conf_pw_b"][0]),
        "gout": nat(i["out_norm_g"][0]), "g2n": nat(i["norm2_g"][0]), "g2p": perm(i["norm2_g"][0]),
        "h1n": nat(i["norm1_g_2"][0]), "h2n": nat(i["norm2_g_2"][0]), "h2p": perm(i["norm2_g_2"][0]),
        "onorm": i["onorm_g_2"][0][:, None],
        "cvec": np.stack([nat(i["c_2"][0]), nat(i["c_ctx_2"])], axis=2).reshape(P, -1),
        "cw2": taps(i["conv_w_2"][0].reshape(9, -1)),
        "rbias": rows(np.concatenate([i["b_group_2"][0], i["b_router_2"][0]])),
        "dtb": rows(i["dt_bias_2"][0]), "alog": rows(i["a_log_2"][0]),
        "io32": rows(np.arange(NE, dtype=f32)), "base0": rows(CAP * np.arange(NE, dtype=f32)),
        "base1": rows(CAP * (NE - 1 - np.arange(NE, dtype=f32))), "io4": rows(np.arange(NG, dtype=f32)),
        "io15": rows(np.arange(NOV, dtype=f32)),
        "tokf": np.arange(T, dtype=f32).reshape(TT, P).T, "slot0": rows(CAP * np.arange(NBLK + 1, dtype=f32)),
        "io64": rows(np.arange(CAP, dtype=f32) - CAP),
    }
    b_mod = i["b_mod_2"][0].reshape(6, D)
    parts["bmc"] = np.concatenate([nat(b_mod[j]) for j in (0, 1, 3, 4)] + [perm(b_mod[j]) for j in (3, 4)]
                                  + [nat(b_mod[j]) for j in (0, 1)], axis=1)
    for name, width in PARAMS:
        assert parts[name].shape == (P, width), (name, parts[name].shape)
    lbd = np.zeros((P, 4, P), f32)
    for g, w in enumerate((i["lru_wa"][0], i["lru_wx"][0])):
        for n in range(4):
            r = HD * (n % 2)
            lbd[r:r + HD, 2 * g + n // 2, r:r + HD] = w[n]
    router = [np.concatenate([i[x][0], i[y][0]], axis=1).reshape(KD, P, NR).transpose(1, 0, 2).reshape(P, -1)
              for x, y in (("router_coarse", "router_fine"), ("w_group_2", "w_router_2"))]
    chan, pos = fourier_tables()
    w_in_2 = i["w_in_2"][0]
    arrays = {
        "par": np.concatenate([parts[n] for n, _ in PARAMS], axis=1),
        "mats": square_matrices(), "csc": chan, "dft": pos, "lbd": lbd.reshape(P, -1),
        "rw": np.concatenate(router, axis=1),
        "gw": w_in_2[:, 2560:].reshape(KD, P, 16).transpose(1, 0, 2).reshape(P, -1),
        "bmod": i["b_mod_2"], "xT": i["x"][0].T, "x": i["x"][0],
        "ctxT": i["ctx_2"][0].T, "w_mod": i["w_mod_2"][0], "w_in": i["w_in"][0], "w_out": i["w_out"][0],
        "pw": i["conf_pw_w"][0], "w_in_2": w_in_2, "w_out_2": i["w_out_2"][0],
        "w_gate": i["exp_w_gate"][0], "w_up": i["exp_w_up"][0], "w_down": i["exp_w_down"][0],
        "w_gate_2": i["w_gate_2"][0], "w_up_2": i["w_up_2"][0], "w_down_2": i["w_down_2"][0],
        "fg": i["final_g_2"][None, :],
    }
    arrays = {n: np.ascontiguousarray(v) for n, v in arrays.items()}
    nc = bacc.Bacc("TRN2", target_bir_lowering=False, num_devices=1)
    aps = {n: nc.dram_tensor(f"in_{n}", v.shape, mybir.dt.from_np(v.dtype), kind="ExternalInput").ap()
           for n, v in arrays.items()}
    out = nc.dram_tensor("out", (T, D), F32, kind="ExternalOutput").ap()
    build(nc, aps, out)
    r = run_bass_kernel_spmd(nc, [{f"in_{n}": v for n, v in arrays.items()}], core_ids=[0])
    return r.results[0]["out"].reshape(1, T, D)
```
